# Optimizing a Trainium2 kernel written in Bass

```python
import jax, jax.numpy as jnp
from jax import lax
import numpy as np

D_MODEL = 1024
BATCH = 1
SEQ = 256
DEPTH = 1
DEC_BATCH = 1
DEC_SEQ = 1024
PAST_LEN = 128

N_META = 16
D_MIX = D_MODEL
HG_WIDTH = D_MIX // 2
HG_HEADS = 4
HG_HEAD_DIM = HG_WIDTH // HG_HEADS
CONV_WIDTH = D_MIX - HG_WIDTH
CONV_KERNEL = 31
CONV_PAD = (CONV_KERNEL - 1) // 2
CHUNK = 32
META_PAD = (-N_META) % CHUNK
D_FF = 2816
FFN_RES = 0.5
Z_WIDTH = 5 * HG_WIDTH + 2 * CONV_WIDTH
RMS_EPS = 1e-6
LN_EPS = 1e-5

kernel_name = 'hymba_hgrn2_conformer_encoder'

def rmsnorm(x, g):
    xf = x.astype(jnp.float32)
    y = xf * lax.rsqrt(jnp.mean(xf * xf, axis=-1, keepdims=True) + RMS_EPS)
    return (y * g.astype(jnp.float32)).astype(x.dtype)

def layernorm(x, g, b):
    xf = x.astype(jnp.float32)
    mu = jnp.mean(xf, axis=-1, keepdims=True)
    xc = xf - mu
    y = xc * lax.rsqrt(jnp.mean(xc * xc, axis=-1, keepdims=True) + LN_EPS)
    return (y * g.astype(jnp.float32) + b.astype(jnp.float32)).astype(x.dtype)

def swiglu(x, w_gate, w_up, w_down):
    return (jax.nn.silu(x @ w_gate) * (x @ w_up)) @ w_down

def gla_chunk_scan(q, k, v, logf):
    n, nh, length, dk = q.shape
    dv = v.shape[-1]
    nc = length // CHUNK

    def to_chunks(a):
        return a.astype(jnp.float32).reshape(n, nh, nc, CHUNK, a.shape[-1]).transpose(2, 0, 1, 3, 4)

    qc, kc, vc, gc = to_chunks(q), to_chunks(k), to_chunks(v), to_chunks(logf)
    tri = jnp.tril(jnp.ones((CHUNK, CHUNK), dtype=bool))

    def step(state, blk):
        qb, kb, vb, gb = blk
        b = jnp.cumsum(gb, axis=2)
        b_last = b[:, :, -1:, :]
        o_inter = jnp.einsum('nhtk,nhkv->nhtv', qb * jnp.exp(b), state)
        diff = b[:, :, :, None, :] - b[:, :, None, :, :]
        decay = jnp.exp(jnp.where(tri[:, :, None], diff, -jnp.inf))
        scores = jnp.einsum('nhtk,nhsk,nhtsk->nhts', qb, kb, decay)
        o_intra = jnp.einsum('nhts,nhsv->nhtv', scores, vb)
        new_state = (jnp.exp(b_last[:, :, 0, :, None]) * state
                     + jnp.einsum('nhsk,nhsv->nhkv', kb * jnp.exp(b_last - b), vb))
        return new_state, o_inter + o_intra

    s0 = jnp.zeros((n, nh, dk, dv), jnp.float32)
    _, out = lax.scan(step, s0, (qc, kc, vc, gc))
    return out.transpose(1, 2, 0, 3, 4).reshape(n, nh, length, dv)

def depthwise_conv(u, w, b):
    y = lax.conv_general_dilated(u, w.astype(u.dtype)[:, None, :], window_strides=(1,),
                                 padding=[(CONV_PAD, CONV_PAD)],
                                 dimension_numbers=('NWC', 'WIO', 'NWC'),
                                 feature_group_count=u.shape[-1])
    return y + b.astype(u.dtype)

def token_mixing(u, w_in, lb, hg_norm, conv_w, conv_b, conv_ln_g, conv_ln_b, w_out):
    bsz, t, _ = u.shape
    W, C = HG_WIDTH, CONV_WIDTH
    z = u @ w_in

    def heads(a):
        return a.reshape(bsz, t, HG_HEADS, HG_HEAD_DIM).transpose(0, 2, 1, 3)

    q = jax.nn.silu(heads(z[..., 0:W])).astype(jnp.float32)
    v = heads(z[..., 3 * W:4 * W]).astype(jnp.float32)
    f_logits = jnp.stack([heads(z[..., W:2 * W]), heads(z[..., 2 * W:3 * W])]).astype(jnp.float32)
    lb = lb.reshape(2, 1, HG_HEADS, 1, HG_HEAD_DIM)
    logf = jnp.logaddexp(jnp.log(lb), jnp.log1p(-lb) + jax.nn.log_sigmoid(f_logits))
    k = -jnp.expm1(logf)

    def pad(a):
        return jnp.pad(a, ((0, 0),) * (a.ndim - 2) + ((META_PAD, 0), (0, 0)))

    def flip(a):
        return jnp.flip(a, axis=-2)

    qp, vp, kp, gp = pad(q), pad(v), pad(k), pad(logf)
    qs = jnp.concatenate([qp, flip(qp)], axis=0)
    vs = jnp.concatenate([vp, flip(vp)], axis=0)
    ks = jnp.concatenate([kp[0], flip(kp[1])], axis=0)
    gs = jnp.concatenate([gp[0], flip(gp[1])], axis=0)
    o = gla_chunk_scan(qs, ks, vs, gs)
    o = (o[:bsz] + flip(o[bsz:]))[:, :, META_PAD:]
    o = o * lax.rsqrt(jnp.mean(o * o, axis=-1, keepdims=True) + RMS_EPS)
    o = o.transpose(0, 2, 1, 3).reshape(bsz, t, W) * hg_norm.astype(jnp.float32)
    hg_out = (o * jax.nn.silu(z[..., 4 * W:5 * W].astype(jnp.float32))).astype(u.dtype)

    glu = z[..., 5 * W:5 * W + C] * jax.nn.sigmoid(z[..., 5 * W + C:5 * W + 2 * C])
    c = depthwise_conv(glu, conv_w, conv_b)
    c = jax.nn.silu(layernorm(c, conv_ln_g, conv_ln_b))

    return jnp.concatenate([hg_out, c], axis=-1) @ w_out

def encoder_trunk(x, meta_tokens, ffn1_norm, ffn1_w_gate, ffn1_w_up, ffn1_w_down, mix_norm, w_in,
                  lb_logits, hg_norm, conv_w, conv_b, conv_ln_g, conv_ln_b, w_out,
                  ffn2_norm, ffn2_w_gate, ffn2_w_up, ffn2_w_down, final_norm):
    bsz = x.shape[0]
    meta = jnp.broadcast_to(meta_tokens[None].astype(x.dtype), (bsz, N_META, x.shape[-1]))
    h = jnp.concatenate([meta, x], axis=1)
    lb_all = jnp.cumsum(jax.nn.softmax(lb_logits.astype(jnp.float32), axis=0), axis=0)
    for layer in range(DEPTH):
        h = h + FFN_RES * swiglu(rmsnorm(h, ffn1_norm[layer]), ffn1_w_gate[layer], ffn1_w_up[layer], ffn1_w_down[layer])
        h = h + token_mixing(rmsnorm(h, mix_norm[layer]), w_in[layer], lb_all[layer], hg_norm[layer],
                             conv_w[layer], conv_b[layer], conv_ln_g[layer], conv_ln_b[layer], w_out[layer])
        h = h + FFN_RES * swiglu(rmsnorm(h, ffn2_norm[layer]), ffn2_w_gate[layer], ffn2_w_up[layer], ffn2_w_down[layer])
    return rmsnorm(h, final_norm)[:, N_META:]

def setup_inputs(seed: int = 0) -> dict:
    key = jax.random.key(seed)
    ks = jax.random.split(key, 24)
    f32 = jnp.float32

    def nrm(k, shape, scale):
        return jax.random.normal(k, shape, f32) * scale

    def gain(k, shape):
        return 1.0 + 0.02 * jax.random.normal(k, shape, f32)

    return {
        'x_prompt': nrm(ks[0], (BATCH, SEQ, D_MODEL), 1.0),
        'x_sample': nrm(ks[1], (DEC_BATCH, DEC_SEQ, D_MODEL), 1.0),
        'meta_tokens': nrm(ks[2], (N_META, D_MODEL), 1.0),
        'ffn1_norm': gain(ks[3], (DEPTH, D_MODEL)),
        'ffn1_w_gate': nrm(ks[4], (DEPTH, D_MODEL, D_FF), D_MODEL ** -0.5),
        'ffn1_w_up': nrm(ks[5], (DEPTH, D_MODEL, D_FF), D_MODEL ** -0.5),
        'ffn1_w_down': nrm(ks[6], (DEPTH, D_FF, D_MODEL), D_FF ** -0.5),
        'mix_norm': gain(ks[7], (DEPTH, D_MODEL)),
        'w_in': nrm(ks[8], (DEPTH, D_MODEL, Z_WIDTH), D_MODEL ** -0.5),
        'lb_logits': nrm(ks[9], (DEPTH + 1, 2, HG_WIDTH), 0.5),
        'hg_norm': gain(ks[10], (DEPTH, HG_WIDTH)),
        'conv_w': nrm(ks[11], (DEPTH, CONV_KERNEL, CONV_WIDTH), CONV_KERNEL ** -0.5),
        'conv_b': nrm(ks[12], (DEPTH, CONV_WIDTH), 0.02),
        'conv_ln_g': gain(ks[13], (DEPTH, CONV_WIDTH)),
        'conv_ln_b': nrm(ks[14], (DEPTH, CONV_WIDTH), 0.02),
        'w_out': nrm(ks[15], (DEPTH, D_MIX, D_MODEL), D_MIX ** -0.5),
        'ffn2_norm': gain(ks[16], (DEPTH, D_MODEL)),
        'ffn2_w_gate': nrm(ks[17], (DEPTH, D_MODEL, D_FF), D_MODEL ** -0.5),
        'ffn2_w_up': nrm(ks[18], (DEPTH, D_MODEL, D_FF), D_MODEL ** -0.5),
        'ffn2_w_down': nrm(ks[19], (DEPTH, D_FF, D_MODEL), D_FF ** -0.5),
        'final_norm': gain(ks[20], (D_MODEL,)),
    }

def reference(x_prompt, x_sample, meta_tokens, ffn1_norm, ffn1_w_gate, ffn1_w_up, ffn1_w_down,
              mix_norm, w_in, lb_logits, hg_norm, conv_w, conv_b, conv_ln_g, conv_ln_b, w_out,
              ffn2_norm, ffn2_w_gate, ffn2_w_up, ffn2_w_down, final_norm):
    y_prompt = encoder_trunk(x_prompt, meta_tokens, ffn1_norm, ffn1_w_gate, ffn1_w_up, ffn1_w_down,
                             mix_norm, w_in, lb_logits, hg_norm, conv_w, conv_b, conv_ln_g, conv_ln_b,
                             w_out, ffn2_norm, ffn2_w_gate, ffn2_w_up, ffn2_w_down, final_norm)
    y_sample = encoder_trunk(x_sample, meta_tokens, ffn1_norm, ffn1_w_gate, ffn1_w_up, ffn1_w_down,
                             mix_norm, w_in, lb_logits, hg_norm, conv_w, conv_b, conv_ln_g, conv_ln_b,
                             w_out, ffn2_norm, ffn2_w_gate, ffn2_w_up, ffn2_w_down, final_norm)
    return (y_prompt, y_sample)


_drawn_inputs = setup_inputs


def setup_inputs(seed=0):
    import zlib

    import numpy as np

    out = dict(_drawn_inputs(seed))
    spreads = {}
    factors = {'ffn1_norm': 6.535,
     'mix_norm': 4.339,
     'lb_logits': 3.378,
     'hg_norm': 23.09,
     'conv_b': 33.768,
     'conv_ln_g': 200.0,
     'conv_ln_b': 200.0,
     'ffn2_norm': 22.413,
     'final_norm': 25.639}
    for name, (base, spread) in spreads.items():
        noise = np.random.default_rng([zlib.crc32(name.encode()), seed]).standard_normal(out[name].shape)
        drawn = base * np.exp(spread * noise) if base else spread * noise
        out[name] = __import__('jax').numpy.asarray(drawn.astype(out[name].dtype))
    for name, factor in factors.items():
        out[name] = (out[name] * factor).astype(out[name].dtype)
    return out
```

```python
from contextlib import ExitStack, contextmanager

import numpy as np

import concourse.bass as bass
from concourse import mybir

F32 = mybir.dt.float32
F32R = mybir.dt.float32r
U8 = mybir.dt.uint8
ACT = mybir.ActivationFunctionType
ALU = mybir.AluOpType

P = 128
META = 16
PROMPT = 256
SAMPLE = 1024
T = META + PROMPT + SAMPLE
DATA = PROMPT + SAMPLE
D = 1024
KD = D // P
DFF = 2816
NF = DFF // P
GROUPS = NF // 2
W = 512
HEADS = 4
NCH = DATA // P
PCH = PROMPT // P
LEVELS = (1, 2, 4, 8, 16, 32, 64)
TAPS = 31
PAD = (TAPS - 1) // 2
RMS_EPS = 1e-6
LN_EPS = 1e-5
BUF = T * 4
GLU_LEN = META + PROMPT + PAD + META + SAMPLE + PAD
GLU_B = (GLU_LEN * 4 + 31) // 32 * 32
COUT_LEN = PROMPT + PAD + META + SAMPLE
GLU_S = META + PROMPT + PAD
RING = 3

G_FFN1, G_MIX, G_FFN2, G_FIN, LB0, LB1, HGN, CB, LNG, LNB, NVEC = 0, 8, 16, 24, 32, 40, 48, 52, 56, 60, 64

CHUNK_PIECES = [(0, 4), (4, 8), (8, 10)]
COL_PIECES = [(0, 512), (512, 1024), (1024, DATA)]
FWD_G = ["meta", 0] + list(range(PCH, NCH - 1))
BWD_G = [1] + list(range(NCH - 1, PCH, -1))
ALL_G = [("f", c) for c in FWD_G] + [("b", c) for c in BWD_G]
G_PIECES = [ALL_G[a:a + 3] for a in range(0, len(ALL_G), 3)]
TF_PIECES = [FWD_G[a:a + 4] for a in range(0, len(FWD_G), 4)]
TB_PIECES = [BWD_G[a:a + 4] for a in range(0, len(BWD_G), 4)]
V_ALL = ["meta"] + list(range(NCH))
V_PIECES = [V_ALL[a:a + 4] for a in range(0, len(V_ALL), 4)]
STAGE = {}
_at = 0
for _name, _n in ([("v", len(V_PIECES)), ("diag", 3)] + [(h, 3) for h in LEVELS]
                  + [("tf", len(TF_PIECES)), ("tb", len(TB_PIECES)), ("g", len(G_PIECES)), ("out", 3), ("ss", 3)]):
    STAGE[_name] = _at
    _at += _n
PIECES = _at
assert PIECES % 2 == 0


def state_f(c):
    return 0 if c == PCH else c


class Count:

    def __init__(self):
        self.fixed, self.i, self.per = 0, None, 0

    def now(self, more=0):
        return self.fixed + more if self.i is None else self.i * self.per + (self.fixed + more)

    def add(self, n=1):
        self.fixed += n


@contextmanager
def looped(eng, start, end, counts):
    at = [c.fixed for c, _ in counts]
    with eng.Fori(start, end) as i:
        for c, per in counts:
            c.i, c.per = i - start, per
        yield i
    for (c, per), a in zip(counts, at):
        assert c.fixed - a == per, (c.fixed - a, per)
        c.i = None
        c.fixed = a + per * (end - start)


def blocks(lo):
    return [(a, min(a + 512, T), a - lo) for a in range(lo, T, 512)]


def encoder(nc, x_prompt, x_sample, meta_tokens, ffn1_norm, ffn1_w_gate, ffn1_w_up, ffn1_w_down, mix_norm,
            w_in, lb_logits, hg_norm, conv_w, conv_b, conv_ln_g, conv_ln_b, w_out, ffn2_norm, ffn2_w_gate,
            ffn2_w_up, ffn2_w_down, final_norm, ident_d, masks_d, y_prompt, y_sample):
    ctx = ExitStack()
    with ctx:
        ctx.enter_context(nc.sbuf_tensor("arena", [P, (SBUF_TOP - SBUF_BASE) // 4 - 8], F32))
        place = [SBUF_BASE]

        def at(name, shape, dt, offset):
            return nc.alloc_sbuf_tensor_at(name, [P] + shape, dt, offset=offset)

        def take(nbytes):
            a = place[0]
            place[0] += (nbytes + 31) // 32 * 32
            assert place[0] <= SBUF_TOP, place[0]
            return a

        o_xh, o_xl = take(KD * BUF), take(KD * BUF)
        XH = at("XH", [KD, T], F32R, o_xh)
        XL = at("XL", [KD, T], F32R, o_xl)
        o_raw = take(RING * 4096)
        WR = at("WR", [RING, 1024], F32, o_raw)
        WH = at("WH", [RING, 1024], F32R, take(RING * 4096))
        WL = at("WL", [RING, 1024], F32R, take(RING * 4096))
        o_r = take(BUF)
        R = at("R", [T], F32, o_r)
        o_h = take(KD * BUF)
        H = at("H", [KD, T], F32, o_h)
        o_hid = take(4 * BUF + 2 * GLU_B)
        o_t1, o_t2 = take(BUF), take(BUF)
        HH = at("HH", [3, T], F32R, o_hid)
        HL = at("HL", [3, T], F32R, o_hid + 3 * BUF)
        T1, T2 = at("T1", [T], F32, o_t1), at("T2", [T], F32, o_t2)
        XT = at("XT", [NCH, D], F32, o_hid)
        XM = at("XM", [D], F32, o_r)
        STG = at("STG", [P], F32, o_xl)
        CWS = at("CWS", [W], F32, o_xl + 512)
        MS = at("MS", [len(LEVELS), P], F32, o_xl + 4096)
        Q, FF, FB, AF, AB, BF, BB, VT = (at(n, [T], F32, o_h + k * BUF)
                                         for k, n in enumerate(("Q", "FF", "FB", "AF", "AB", "BF", "BB", "VT")))
        VTOK, GS, SC, KS = (at(n, [T], F32, o_hid + k * BUF) for k, n in enumerate(("VTOK", "GS", "SC", "KS")))
        GLU = at("GLU", [GLU_LEN], F32, o_hid + 4 * BUF)
        COUT = at("COUT", [GLU_LEN], F32, o_hid + 4 * BUF + GLU_B)
        CR = at("CR", [4, T], F32, o_hid)
        small = {}
        for n, shape, dt, size in (("ident", [P], F32, 4), ("ones", [P], F32, 4), ("masks", [len(LEVELS), P], U8, 1),
                                   ("VM", [P], F32, 4), ("COL", [NVEC], F32, 4), ("CWT", [4, TAPS], F32, 4),
                                   ("LB", [8], F32, 4), ("OLB", [8], F32, 4), ("LBM", [8], F32, 4),
                                   ("FL", [2, NCH], F32, 4)):
            small[n] = at(n, shape, dt, take(int(np.prod(shape)) * size))
        ident, ones, masks, VM, COL, CWT, LB, OLB, LBM, FL = (small[n] for n in (
            "ident", "ones", "masks", "VM", "COL", "CWT", "LB", "OLB", "LBM", "FL"))
        PS = ctx.enter_context(nc.psum_tensor("PS", [P, 4096], F32))
        SET = [PS[:, 0:1536], PS[:, 1536:3072]]
        CB_ = [PS[:, 3072:3584], PS[:, 3584:4096]]

        hsave = nc.dram_tensor("hsave", [KD, P, T], F32, kind="Internal").ap()
        ysave = nc.dram_tensor("ysave", [HEADS, P, DATA], F32, kind="Internal").ap()
        csave = nc.dram_tensor("csave", [HEADS, P, DATA], F32, kind="Internal").ap()

        def sem(name):
            return ctx.enter_context(nc.semaphore(name))

        raw_loaded = [sem(f"raw_loaded{s}") for s in range(RING)]
        split_hi = [sem(f"split_hi{s}") for s in range(RING)]
        split_lo = [sem(f"split_lo{s}") for s in range(RING)]
        t_full = [sem(f"t_full{s}") for s in range(2)]
        t_free = [sem(f"t_free{s}") for s in range(2)]
        c_full = [sem(f"c_full{s}") for s in range(2)]
        c_free = [sem(f"c_free{s}") for s in range(2)]
        x_loaded = [sem(f"x_loaded{t}") for t in range(NCH + 1)]
        const_loaded, cw_loaded, masks_loaded = sem("const_loaded"), sem("cw_loaded"), sem("masks_loaded")
        ones_set, lb_exp, lb_step, pad_set = (sem(n) for n in (
            "ones_set", "lb_exp", "lb_step", "pad_set"))
        sq_ready, acc_ready, xh_ready, xl_ready, rms_ready, r_ready = (sem(n) for n in (
            "sq_ready", "acc_ready", "xh_ready", "xl_ready", "rms_ready", "r_ready"))
        silu_ready, prod_ready, hid_hi, hid_lo = (sem(n) for n in ("silu_ready", "prod_ready", "hid_hi", "hid_lo"))
        h_saved, h_back, y_saved, c_saved, c_back = (sem(n) for n in ("h_saved", "h_back", "y_saved", "c_saved", "c_back"))
        yb_back = [sem("yb_back0"), sem("yb_back1")]
        (glu_sig, glu_ready, conv_ready, q_sig, q_ready, f_sig, kf_raw, kf_ready, f_ready, fb_sig, kb_raw, kb_ready,
         fb_ready, g_sig, bks_ready, osq_ready, orms_ready, ors_ready, yn_ready, y_ready) = (sem(n) for n in (
             "glu_sig", "glu_ready", "conv_ready", "q_sig", "q_ready", "f_sig", "kf_raw", "kf_ready", "f_ready",
             "fb_sig", "kb_raw", "kb_ready", "fb_ready", "g_sig", "bks_ready", "osq_ready", "orms_ready",
             "ors_ready", "yn_ready", "y_ready"))
        sc_free = sem("sc_free")
        sp_passed, dve_passed = sem("sp_passed"), sem("dve_passed")
        level_up, tap_done, state_step = sem("level_up"), sem("tap_done"), sem("state_step")
        csum, cxc, csq, cacc, cn, csig, caff, cact = (sem(n) for n in (
            "csum", "cxc", "csq", "cacc", "cn", "csig", "caff", "cact"))
        fin_ready, out_stored = sem("fin_ready"), sem("out_stored")
        out_full = [sem("out_full0"), sem("out_full1")]

        block = ctx.enter_context(nc.Block())

        HEAD_SLOTS = [0, 1, 2, 0, 1, 2, 1]
        FFN_UNITS = 6 * GROUPS
        OUT_SLOTS = [n % RING for n in range(KD)]
        FFN1_S0, FFN2_S0 = 0, KD % RING

        def ffn_counts(uses, tiles=None):
            return [(u, 4) for u in uses] + [(t, 12) for t in tiles or []]

        def head_counts(uses, tiles=None):
            return ([(u, HEAD_SLOTS.count(s)) for s, u in enumerate(uses)]
                    + [(t, 4 - s) for s, t in enumerate(tiles or [])])

        @block.sync
        def _(sp):
            for t in range(NCH):
                src = x_prompt[0, t * P:(t + 1) * P, :] if t < PCH else x_sample[0, (t - PCH) * P:(t - PCH + 1) * P, :]
                sp.dma_start(XT[:, t, :], src).then_inc(x_loaded[t], 16)
            uses = [Count() for _ in range(RING)]

            def load(s, src, dst):
                sp.wait_ge(split_hi[s], uses[s].now())
                sp.wait_ge(split_lo[s], uses[s].now())
                sp.sem_inc(sp_passed, 1)
                sp.dma_start(dst(WR[:, s, :]), src).then_inc(raw_loaded[s], 16)
                uses[s].add()

            cols = lambda w: w[0].rearrange("(k p) n -> p k n", p=P)
            by_k = lambda v: v.rearrange("p (k n) -> p k n", k=KD)

            def ffn(w_gate, w_up, w_down, s0):
                n = [s0]

                def nxt():
                    n[0] += 1
                    return (n[0] - 1) % RING

                def gate_up(m):
                    for w in (w_gate, w_up):
                        load(nxt(), cols(w)[:, :, bass.ds(m * P, P)], by_k)

                def down(j):
                    rows = w_down[0].rearrange("(g c p) n -> g p c n", c=2, p=P)
                    for half in range(2):
                        src = rows[bass.ds(j, 1), :, :, half * 512:(half + 1) * 512].rearrange("g p c n -> (g p) c n")
                        load(nxt(), src, lambda v: v.rearrange("p (c n) -> p c n", c=2))

                def group(j):
                    gate_up(2 * j)
                    down(j - 1)
                    gate_up(2 * j + 1)

                gate_up(0)
                gate_up(1)
                with looped(sp, 0, (GROUPS - 1) // 2, ffn_counts(uses)) as t:
                    group(2 * t + 1)
                    group(2 * t + 2)
                down(GROUPS - 1)

            ffn(ffn1_w_gate, ffn1_w_up, ffn1_w_down, FFN1_S0)

            def head_units(i):
                for s, c in zip(HEAD_SLOTS, (5, 6, 3, 0, 1, 2, 4)):
                    load(s, cols(w_in)[:, :, bass.ds(i * P + c * W, P)], by_k)

            with looped(sp, 0, HEADS, head_counts(uses)) as i:
                head_units(i)
            for n in range(KD):
                load(OUT_SLOTS[n], cols(w_out)[:, :, n * P:(n + 1) * P], by_k)
            ffn(ffn2_w_gate, ffn2_w_up, ffn2_w_down, FFN2_S0)
            for t in range(NCH):
                sp.wait_ge(out_full[(t + 1) % 2], t // 2 + 1)
                dst = y_prompt[0, t * P:(t + 1) * P, :] if t < PCH else y_sample[0, (t - PCH) * P:(t - PCH + 1) * P, :]
                sp.dma_start(dst, XT[:, t, :]).then_inc(out_stored, 16)
            sp.wait_ge(out_stored, 16 * NCH)

        @block.gpsimd
        def _(pool):
            pool.memset(ones[:], 1.0).then_inc(ones_set, 1)
            pool.sem_inc(sc_free, 1)
            pool.dma_start(ident[:], ident_d).then_inc(const_loaded, 16)
            for row, src in ((G_FFN1, ffn1_norm), (G_MIX, mix_norm), (G_FFN2, ffn2_norm),
                             (HGN, hg_norm), (CB, conv_b), (LNG, conv_ln_g), (LNB, conv_ln_b)):
                n = src.shape[1] // P
                pool.dma_start(STG[row:row + n, :], src.rearrange("a (k p) -> (a k) p", p=P)).then_inc(const_loaded, 16)
            pool.dma_start(STG[G_FIN:G_FIN + KD, :], final_norm.rearrange("(k p) -> k p", p=P)).then_inc(const_loaded, 16)
            pool.dma_start(STG[LB0:LB0 + 16, :], lb_logits.rearrange("l d (h p) -> (l d h) p", p=P)).then_inc(const_loaded, 16)
            pool.dma_start(XM[0:META, :], meta_tokens).then_inc(x_loaded[NCH], 16)
            pool.dma_start(CWS[0:TAPS, :], conv_w[0]).then_inc(cw_loaded, 16)
            pool.dma_start(MS[:], masks_d).then_inc(masks_loaded, 16)
            for k in range(KD):
                pool.wait_ge(sq_ready, KD + k + 1)
                pool.dma_start(hsave[k], H[:, k, :]).then_inc(h_saved, 16)

            def save_c(i):
                pool.wait_ge(conv_ready, i + 1)
                pool.dma_start(csave[bass.ds(i, 1), :, 0:PROMPT].rearrange("a p n -> (a p) n"),
                               COUT[:, 0:PROMPT]).then_inc(c_saved, 16)
                pool.dma_start(csave[bass.ds(i, 1), :, PROMPT:DATA].rearrange("a p n -> (a p) n"),
                               COUT[:, COUT_LEN - SAMPLE:COUT_LEN]).then_inc(c_saved, 16)

            def save_y(i):
                pool.wait_ge(y_ready, i + 1)
                pool.dma_start(ysave[bass.ds(i, 1), :, :].rearrange("a p n -> (a p) n"),
                               SC[:, META:T]).then_inc(y_saved, 16)
                pool.wait_ge(y_saved, 16 * (i + 1))
                pool.sem_inc(sc_free, 1)

            save_c(0)
            with pool.Fori(1, HEADS) as i:
                save_y(i - 1)
                save_c(i)
            save_y(HEADS - 1)
            pool.wait_ge(c_saved, 32 * HEADS)
            for n in range(4):
                pool.dma_start(CR[:, n, 0:DATA], csave[n]).then_inc(c_back, 16)
            for k in range(KD):
                pool.dma_start(H[:, k, META:T], hsave[k][:, META:T]).then_inc(h_back, 16)
            for i in range(HEADS):
                if i >= 2:
                    pool.wait_ge(xl_ready, KD * 2 + 4 + i - 1)
                dst = (GLU, COUT)[i % 2]
                pool.dma_start(dst[:, 0:DATA], ysave[i]).then_inc(yb_back[i % 2], 16)

        @block.tensor
        def _(pe):
            uses = [Count() for _ in range(RING)]
            tiles = [Count(), Count()]

            def claim(s):
                pe.wait_ge(t_free[s], tiles[s].now())
                tiles[s].add()

            def unit(s):
                pe.wait_ge(split_lo[s], uses[s].now(1))
                uses[s].add()

            def product(s, wat, xh, xl, cols, first, last):
                for wt, xs in ((WH, (xh, xl)), (WL, (xh,))):
                    for x in xs:
                        for a, b, o in cols:
                            mm = nc.tensor.matmul(SET[s][:, o:o + b - a], wt[:, wat[0], wat[1]:wat[1] + P], x(a, b),
                                                  start=first and wt is WH and x is xh, stop=last and wt is WL)
                return mm

            def columns_in(count0):
                for t in range(-1, NCH):
                    s = (t + 1) % 2
                    pe.wait_ge(x_loaded[t if t >= 0 else NCH], 16)
                    claim(s)
                    for k in range(KD):
                        if t < 0:
                            mm = nc.tensor.transpose(SET[s][:, k * META:(k + 1) * META], XM[0:META, k * P:(k + 1) * P],
                                                     ident[0:META, 0:META])
                        else:
                            mm = nc.tensor.transpose(SET[s][:, k * P:(k + 1) * P], XT[:, t, k * P:(k + 1) * P], ident[:])
                    mm.then_inc(t_full[s], 1)

            def sumsq(n, lo, s):
                pe.wait_ge(acc_ready, (KD - 1) * (n + 1))
                claim(s)
                for a, b, o in blocks(lo):
                    mm = nc.tensor.matmul(SET[s][:, o:o + b - a], ones[:], T2[:, a:b], start=True, stop=True)
                mm.then_inc(t_full[s], 1)

            def x_unit(slot, s, lo, norm=None):
                unit(slot)
                claim(s)
                for k in range(KD):
                    if norm is not None:
                        pe.wait_ge(xl_ready, KD * norm + k + 1)
                    mm = product(s, (slot, k * P), lambda a, b: XH[:, k, a:b], lambda a, b: XL[:, k, a:b],
                                 blocks(lo), k == 0, k == KD - 1)
                    if k == KD - 1:
                        mm.then_inc(t_full[s], 1)

            def ffn(lo, s0, xnorm, hid0):
                n = [s0]

                def nxt():
                    n[0] += 1
                    return (n[0] - 1) % RING

                def gate_up(norm=None):
                    x_unit(nxt(), 0, lo, norm)
                    if norm is not None:
                        sumsq(0 if norm == 0 else 2, lo, 1)
                    x_unit(nxt(), 1, lo)

                def down(even, chunks):
                    pe.wait_ge(hid_lo, chunks)
                    for half in range(2):
                        slot = nxt()
                        unit(slot)
                        for q in range(4):
                            s = q % 2
                            claim(s)
                            for c, hs in enumerate((even, 2)):
                                mm = product(s, (slot, c * 512 + q * P), lambda a, b: HH[:, hs, a:b],
                                             lambda a, b: HL[:, hs, a:b], blocks(lo), c == 0, c == 1)
                            mm.then_inc(t_full[s], 1)

                gate_up(xnorm)
                gate_up()
                with looped(pe, 0, (GROUPS - 1) // 2, ffn_counts(uses, tiles)) as t:
                    for g in range(2):
                        gate_up()
                        down(g, t * 4 + (hid0 + 2 * g + 2))
                        gate_up()
                down((GROUPS - 1) % 2, hid0 + NF)

            def chunk_cols(c):
                return (0, META) if c == "meta" else (META + c * P, META + (c + 1) * P)

            def rec(stage, h):
                base = h * (PIECES // 2)

                def piece(name, n):
                    q = STAGE[name] + n
                    pe.wait_ge(c_free[q % 2], base + (q // 2 + 1))
                    return CB_[q % 2], c_full[q % 2]

                def before(name):
                    for q in (STAGE[name] - 2, STAGE[name] - 1):
                        pe.wait_ge(c_free[q % 2], base + (q // 2 + 2))

                if stage == 0:
                    pe.wait_ge(bks_ready, h + 1)
                    for n, cs in enumerate(V_PIECES):
                        bank, full = piece("v", n)
                        for j, c in enumerate(cs):
                            a, b = chunk_cols(c)
                            mm = nc.tensor.transpose(bank[0:b - a, j * P:(j + 1) * P], VT[:, a:b], ident[:])
                        mm.then_inc(full, 1)
                    for n, (c0, c1) in enumerate(CHUNK_PIECES):
                        bank, full = piece("diag", n)
                        for c in range(c0, c1):
                            a, b = chunk_cols(c)
                            mm = nc.tensor.matmul(bank[:, (c - c0) * P:(c - c0 + 1) * P], KS[:, a:b], Q[:, a:b],
                                                  start=True, stop=True)
                        mm.then_inc(full, 1)
                if stage < len(LEVELS):
                    hh = LEVELS[stage]
                    if stage:
                        pe.wait_ge(level_up, 7 * h + stage)
                    for n, (c0, c1) in enumerate(CHUNK_PIECES):
                        bank, full = piece(hh, n)
                        for c in range(c0, c1):
                            a, b = chunk_cols(c)
                            out = bank[:, (c - c0) * P:(c - c0 + 1) * P].rearrange("p (n two h) -> p n two h", two=2, h=hh)
                            for A, B, half in ((AF, BF, 1), (AB, BB, 0)):
                                rhs = B[:, a:b].rearrange("p (n two h) -> p n two h", two=2, h=hh)
                                mm = nc.tensor.matmul(out[:, :, half, :], A[:, a:b], rhs[:, :, half, :],
                                                      start=True, stop=True)
                        mm.then_inc(full, 1)
                if stage == 7:
                    pe.wait_ge(level_up, 7 * h + 7)
                    for name, pieces, A in (("tf", TF_PIECES, AF), ("tb", TB_PIECES, AB)):
                        for n, cs in enumerate(pieces):
                            bank, full = piece(name, n)
                            for j, c in enumerate(cs):
                                a, b = chunk_cols(c)
                                mm = nc.tensor.transpose(bank[0:b - a, j * P:(j + 1) * P], A[:, a:b], ident[:])
                            mm.then_inc(full, 1)
                if stage == 8:
                    before("g")
                    for n, gs in enumerate(G_PIECES):
                        bank, full = piece("g", n)
                        for j, (d, c) in enumerate(gs):
                            order = FWD_G if d == "f" else BWD_G
                            at_ = (FF if d == "f" else FB)[:, order.index(c) * P:(order.index(c) + 1) * P]
                            if c == "meta":
                                mm = nc.tensor.matmul(bank[:, j * P:(j + 1) * P], at_[0:META, :], VM[0:META, :],
                                                      start=True, stop=True)
                            else:
                                mm = nc.tensor.matmul(bank[:, j * P:(j + 1) * P], at_, VTOK[:, c * P:(c + 1) * P],
                                                      start=True, stop=True)
                        mm.then_inc(full, 1)
                if stage == 9:
                    before("out")
                    for n, (c0, c1) in enumerate(CHUNK_PIECES):
                        bank, full = piece("out", n)
                        for c in range(c0, c1):
                            a, b = chunk_cols(c)
                            out = bank[:, (c - c0) * P:(c - c0 + 1) * P]
                            last = c in (PCH - 1, NCH - 1)
                            nc.tensor.matmul(out, VTOK[:, c * P:(c + 1) * P], SC[:, a:b], start=True, stop=False)
                            mm = nc.tensor.matmul(out, KS[:, state_f(c) * P:(state_f(c) + 1) * P], BF[:, a:b],
                                                  start=False, stop=last)
                            if not last:
                                mm = nc.tensor.matmul(out, AF[:, c * P:(c + 1) * P], BB[:, a:b], start=False, stop=True)
                        mm.then_inc(full, 1)
                if stage == 10:
                    pe.wait_ge(osq_ready, h + 1)
                    for n, (a, b) in enumerate(COL_PIECES):
                        bank, full = piece("ss", n)
                        nc.tensor.matmul(bank[:, 0:b - a], ones[:], SC[:, META + a:META + b],
                                         start=True, stop=True).then_inc(full, 1)

            pe.wait_ge(const_loaded, 16 * 10)
            claim(0)
            nc.tensor.transpose(SET[0][:, 0:NVEC], STG[0:NVEC, :], ident[0:NVEC, 0:NVEC]).then_inc(t_full[0], 1)
            pe.wait_ge(cw_loaded, 16)
            claim(1)
            for i in range(4):
                mm = nc.tensor.transpose(SET[1][:, i * TAPS:(i + 1) * TAPS], CWS[0:TAPS, i * P:(i + 1) * P],
                                         ident[0:TAPS, 0:TAPS])
            mm.then_inc(t_full[1], 1)
            columns_in(0)
            pe.wait_ge(ones_set, 1)
            ffn(0, FFN1_S0, 0, 0)

            def head(i, z, r):
                for pos in range(7):
                    slot = HEAD_SLOTS[pos] if z else None
                    s = pos % 2
                    lo = META if pos in (3, 5, 6) else 0
                    first = z == "first" and pos == 0
                    if z:
                        unit(slot)
                    for half in range(2):
                        if r:
                            rec(2 * pos + half, i - 1)
                        if z:
                            if half == 0:
                                claim(s)
                            for k in range(4 * half, 4 * half + 4):
                                if first:
                                    pe.wait_ge(xl_ready, KD + k + 1)
                                mm = product(s, (slot, k * P), lambda a, b: XH[:, k, a:b], lambda a, b: XL[:, k, a:b],
                                             blocks(lo), k == 0, k == KD - 1)
                    if z:
                        mm.then_inc(t_full[s], 1)
                    if first:
                        sumsq(1, 0, 1)

            head(0, "first", False)
            with looped(pe, 1, HEADS, head_counts(uses, tiles)) as i:
                head(i, "z", True)
            head(HEADS, None, True)

            for n, (ready, src) in enumerate(((csum, T1), (cacc, T2))):
                pe.wait_ge(ready, 3)
                claim(1 - n)
                for a, b in COL_PIECES:
                    mm = nc.tensor.matmul(SET[1 - n][:, a:b], ones[:], src[:, META + a:META + b], start=True, stop=True)
                mm.then_inc(t_full[1 - n], 1)
            pe.wait_ge(xl_ready, 3 * KD)
            for n in range(KD):
                x_unit(OUT_SLOTS[n], n % 2, META)
            ffn(META, FFN2_S0, 3, NF)
            sumsq(3, META, 0)
            for t in range(NCH):
                s = (t + 1) % 2
                if t < 2:
                    claim(s)
                else:
                    pe.wait_ge(out_full[s], t // 2)
                for k in range(KD):
                    if t == 0:
                        pe.wait_ge(fin_ready, k + 1)
                    mm = nc.tensor.transpose(SET[s][:, k * P:(k + 1) * P], H[:, k, META + t * P:META + (t + 1) * P], ident[:])
                mm.then_inc(t_full[s], 1)

        @block.scalar
        def _(act):
            uses = [Count() for _ in range(RING)]
            tiles = [Count(), Count()]

            def split(s, settled=True):
                act.wait_ge(raw_loaded[s], uses[s].now(1) * 16)
                if settled:
                    for b in range(2):
                        act.wait_ge(t_full[b], tiles[b].now())
                nc.scalar.activation(WH[:, s, :], WR[:, s, :], ACT.Copy).then_inc(split_hi[s], 1)
                uses[s].add()

            def sqrt_r(s, lo):
                tiles[s].add()
                act.wait_ge(t_free[s], tiles[s].now())
                nc.scalar.activation(T1[:, lo:T], R[:, lo:T], ACT.Sqrt).then_inc(rms_ready, 1)

            def gained(k, lo, gain):
                nc.scalar.activation(XH[:, k, lo:T], H[:, k, lo:T], ACT.Copy,
                                     scale=COL[:, gain + k:gain + k + 1]).then_inc(xh_ready, 1)

            def squared(n, k, lo):
                if k >= 2:
                    act.wait_ge(acc_ready, (KD - 1) * n + k - 1)
                nc.scalar.activation((T1 if k else T2)[:, lo:T], H[:, k, lo:T], ACT.Square).then_inc(sq_ready, 1)

            def ffn(lo, s0, hid0, final_norm_, gain, more):
                n = [s0 + 1]

                def nxt():
                    n[0] += 1
                    return (n[0] - 1) % RING

                def gate_up(hs, chunk, first=False):
                    split(nxt())
                    if first:
                        sqrt_r(1, lo)
                    tiles[0].add()
                    act.wait_ge(t_free[0], tiles[0].now())
                    nc.scalar.activation(T2[:, lo:T], T1[:, lo:T], ACT.Silu).then_inc(silu_ready, 1)
                    split(nxt())
                    tiles[1].add()
                    act.wait_ge(prod_ready, chunk + 1)
                    nc.scalar.activation(HH[:, hs, lo:T], T2[:, lo:T], ACT.Copy).then_inc(hid_hi, 1)

                gate_up(0, hid0, True)
                gate_up(2, hid0 + 1)
                with looped(act, 0, (GROUPS - 1) // 2, ffn_counts(uses, tiles)) as t:
                    for g in range(2):
                        gate_up(1 - g, t * 4 + (hid0 + 2 * g + 2))
                        for half in range(2):
                            split(nxt())
                            for b in range(2):
                                tiles[b].add(2)
                        gate_up(2, t * 4 + (hid0 + 2 * g + 3))
                for half in range(2):
                    if half == 0 or more:
                        split(nxt())
                    for q in range(4):
                        b, k = q % 2, 4 * half + q
                        tiles[b].add()
                        act.wait_ge(t_free[b], tiles[b].now())
                        if gain is not None:
                            gained(k, lo, gain)
                        squared(final_norm_, k, lo)

            act.wait_ge(lb_step, 3)
            nc.scalar.activation(LB[:], LB[:], ACT.Exp).then_inc(lb_exp, 1)
            nc.scalar.activation(OLB[:], OLB[:], ACT.Exp).then_inc(lb_exp, 1)
            tiles[0].add()
            tiles[1].add()
            for t in range(-1, NCH):
                s = (t + 1) % 2
                tiles[s].add()
                if s == 1:
                    act.wait_ge(t_full[s], tiles[s].now())
                    nc.scalar.activation(H[:, :, META + t * P:META + (t + 1) * P],
                                         SET[s][:, 0:D].rearrange("p (k n) -> p k n", k=KD), ACT.Copy).then_inc(t_free[s], 1)
            split(FFN1_S0, settled=False)
            act.wait_ge(t_free[0], tiles[0].now())
            act.wait_ge(t_free[1], tiles[1].now())
            for k in range(KD):
                gained(k, 0, G_FFN1)
                squared(0, k, 0)
            ffn(0, FFN1_S0, 0, 1, G_MIX, True)

            def rec(stage, h):
                base = h * (PIECES // 2)

                def piece(name, n):
                    q = STAGE[name] + n
                    act.wait_ge(c_full[q % 2], base + (q // 2 + 1))
                    return CB_[q % 2], c_free[q % 2]

                def read_out(name):
                    last = STAGE[name] + 2
                    for q in (last - 1, last):
                        act.wait_ge(c_free[q % 2], base + (q // 2 + 2))

                if stage == 0:
                    for n, cs in enumerate(V_PIECES):
                        bank, free = piece("v", n)
                        if cs[0] == "meta":
                            nc.scalar.activation(VM[0:META, :], bank[0:META, 0:P], ACT.Copy)
                            cs, bank = cs[1:], bank[:, P:512]
                        nc.scalar.activation(VTOK[:, cs[0] * P:(cs[-1] + 1) * P], bank[:, 0:len(cs) * P],
                                             ACT.Copy).then_inc(free, 1)
                if stage == 7:
                    for name, pieces, dst in (("tf", TF_PIECES, FF), ("tb", TB_PIECES, FB)):
                        for n, cs in enumerate(pieces):
                            bank, free = piece(name, n)
                            at0 = n * 4 * P
                            if cs[0] == "meta":
                                nc.scalar.activation(dst[0:META, 0:P], bank[0:META, 0:P], ACT.Copy)
                                cs, at0, bank = cs[1:], at0 + P, bank[:, P:512]
                            nc.scalar.activation(dst[:, at0:at0 + len(cs) * P], bank[:, 0:len(cs) * P],
                                                 ACT.Copy).then_inc(free, 1)
                if stage == 9:
                    for n, (c0, c1) in enumerate(CHUNK_PIECES):
                        bank, free = piece("out", n)
                        nc.scalar.activation(AB[:, META + c0 * P:META + c1 * P], bank[:, 0:(c1 - c0) * P],
                                             ACT.Copy).then_inc(free, 1)
                if stage == 10:
                    read_out("out")
                    nc.scalar.activation(SC[:, META:T], AB[:, META:T], ACT.Square).then_inc(osq_ready, 1)
                    read_out("ss")
                    nc.scalar.activation(KS[:, META:T], KS[:, META:T], ACT.Sqrt).then_inc(orms_ready, 1)

            def head(i, z, r):
                for pos in range(7):
                    s = pos % 2
                    if r:
                        rec(2 * pos, i - 1)
                    if z:
                        split((HEAD_SLOTS + HEAD_SLOTS[0:1])[pos + 1])
                        tiles[s].add()
                    if z == "first" and pos == 0:
                        sqrt_r(1, 0)
                    if r:
                        rec(2 * pos + 1, i - 1)
                    if not z:
                        continue
                    if pos in (1, 3, 4, 5, 6):
                        act.wait_ge(t_free[s], tiles[s].now())
                    if pos == 1:
                        nc.scalar.activation(T2[:], T2[:], ACT.Sigmoid).then_inc(glu_sig, 1)
                    if pos == 3:
                        nc.scalar.activation(T2[:, META:T], T1[:, META:T], ACT.Sigmoid).then_inc(q_sig, 1)
                    if pos == 4:
                        forget(i, 0, AF, f_sig, kf_raw, kf_ready, 0)
                    if pos == 5:
                        act.wait_ge(y_ready, i)
                        forget(i, META, AB, fb_sig, kb_raw, kb_ready, HEADS)
                    if pos == 6:
                        nc.scalar.activation(T2[:, META:T], T1[:, META:T], ACT.Sigmoid).then_inc(g_sig, 1)

            def forget(i, lo, A, sig, raw, ready, ld):
                nc.scalar.activation(T2[:, lo:T], T1[:, lo:T], ACT.Sigmoid).then_inc(sig, 1)
                nc.scalar.activation(A[:, lo:T], T1[:, lo:T], ACT.Sigmoid, scale=-1.0).then_inc(raw, 1)
                act.wait_ge(raw, i + 1)
                olb = OLB[:, i + ld:i + ld + 1] if isinstance(i, int) else OLB[:, bass.ds(i + ld, 1)]
                nc.scalar.activation(A[:, lo:T], A[:, lo:T], ACT.Copy, scale=olb).then_inc(ready, 1)

            act.wait_ge(h_saved, 16 * KD)
            head(0, "first", False)
            with looped(act, 1, HEADS, head_counts(uses, tiles)) as i:
                head(i, "z", True)
            head(HEADS, None, True)

            for n in range(4):
                if n < 3:
                    act.wait_ge(cxc, n + 1)
                else:
                    act.wait_ge(t_free[1], tiles[1].now(1))
                if n >= 2:
                    act.wait_ge(cacc, n - 1)
                nc.scalar.activation((T1 if n else T2)[:, META:T], CR[:, n, 0:DATA], ACT.Square).then_inc(csq, 1)
            tiles[0].add()
            tiles[1].add()
            act.wait_ge(t_free[0], tiles[0].now())
            nc.scalar.activation(T1[:, META:T], T1[:, META:T], ACT.Sqrt).then_inc(rms_ready, 1)
            for n in range(4):
                act.wait_ge(cn, n + 1)
                if n:
                    act.wait_ge(cact, n)
                nc.scalar.activation(T2[:, META:T], CR[:, n, 0:DATA], ACT.Sigmoid, scale=COL[:, LNG + n:LNG + n + 1],
                                     bias=COL[:, LNB + n:LNB + n + 1]).then_inc(csig, 1)
                act.wait_ge(cact, n + 1)
                nc.scalar.activation(XH[:, 4 + n, META:T], CR[:, n, 0:DATA], ACT.Copy).then_inc(xh_ready, 1)
            for n in range(HEADS):
                act.wait_ge(yb_back[n % 2], 16 * (n // 2 + 1))
                nc.scalar.activation(XH[:, n, META:T], (GLU, COUT)[n % 2][:, 0:DATA], ACT.Copy).then_inc(xh_ready, 1)
            act.wait_ge(xl_ready, 3 * KD)
            for n in range(KD):
                split((OUT_SLOTS + [FFN2_S0])[n + 1])
                tiles[n % 2].add()
                act.wait_ge(t_free[n % 2], tiles[n % 2].now())
                squared(2, n, META)
            for k in range(KD):
                gained(k, META, G_FFN2)
            ffn(META, FFN2_S0, NF, 3, None, False)
            sqrt_r(0, META)
            for t in range(0, NCH, 2):
                act.wait_ge(t_full[1], tiles[1].now(t // 2 + 1))
                nc.scalar.activation(XT[:, t, :], SET[1][:, 0:D], ACT.Copy).then_inc(out_full[1], 1)

        @block.vector
        def _(dve):
            uses = [Count() for _ in range(RING)]
            tiles = [Count(), Count()]
            tt, stt, ts = nc.vector.tensor_tensor, nc.vector.scalar_tensor_tensor, nc.vector.tensor_scalar

            def split(s):
                uses[s].add()
                dve.wait_ge(split_hi[s], uses[s].now())
                tt(WL[:, s, :], WR[:, s, :], WH[:, s, :].bitcast(F32), ALU.subtract).then_inc(split_lo[s], 1)

            def tile(s):
                tiles[s].add()
                dve.wait_ge(t_full[s], tiles[s].now())

            def inverse_rms(n, s, lo):
                tile(s)
                ts(R[:, lo:T], SET[s][:, 0:T - lo], 1.0 / D, RMS_EPS, ALU.mult, ALU.add).then_inc(t_free[s], 1)
                dve.wait_ge(rms_ready, n + 1)
                nc.vector.reciprocal(R[:, lo:T], T1[:, lo:T]).then_inc(r_ready, 1)
                dve.wait_ge(r_ready, n + 1)

            def low_part(k, lo, gain, count):
                dve.wait_ge(xh_ready, count)
                stt(XL[:, k, lo:T], H[:, k, lo:T], COL[:, gain + k:gain + k + 1], XH[:, k, lo:T].bitcast(F32),
                    ALU.mult, ALU.subtract).then_inc(xl_ready, 1)

            def add_square(n, k, lo):
                if k:
                    dve.wait_ge(sq_ready, KD * n + k + 1)
                    if k >= 2:
                        dve.wait_ge(acc_ready, (KD - 1) * n + k - 1)
                    tt(T2[:, lo:T], T2[:, lo:T], T1[:, lo:T], ALU.add).then_inc(acc_ready, 1)

            def ffn(lo, s0, hid0, roots, final_norm_, gain, xcount, more):
                n = [s0 + 1]
                cols = T - lo

                def nxt():
                    n[0] += 1
                    return (n[0] - 1) % RING

                def gate_up(hs, chunk, first=False):
                    split(nxt())
                    if first:
                        inverse_rms(roots, 1, lo)
                    tile(0)
                    tt(T1[:, lo:T], SET[0][:, 0:cols], R[:, lo:T], ALU.mult).then_inc(t_free[0], 1)
                    split(nxt())
                    tile(1)
                    dve.wait_ge(silu_ready, chunk + 1)
                    tt(T1[:, lo:T], SET[1][:, 0:cols], R[:, lo:T], ALU.mult).then_inc(t_free[1], 1)
                    dve.wait_ge(t_free[1], tiles[1].now())
                    tt(T2[:, lo:T], T2[:, lo:T], T1[:, lo:T], ALU.mult).then_inc(prod_ready, 1)
                    dve.wait_ge(hid_hi, chunk + 1)
                    tt(HL[:, hs, lo:T], T2[:, lo:T], HH[:, hs, lo:T].bitcast(F32), ALU.subtract).then_inc(hid_lo, 1)

                def residual(k):
                    tile(k % 2)
                    stt(H[:, k, lo:T], SET[k % 2][:, 0:cols], 0.5, H[:, k, lo:T], ALU.mult, ALU.add).then_inc(t_free[k % 2], 1)

                gate_up(0, hid0, True)
                gate_up(2, hid0 + 1)
                with looped(dve, 0, (GROUPS - 1) // 2, ffn_counts(uses, tiles)) as t:
                    for g in range(2):
                        gate_up(1 - g, t * 4 + (hid0 + 2 * g + 2))
                        for half in range(2):
                            split(nxt())
                            for q in range(4):
                                residual(4 * half + q)
                        gate_up(2, t * 4 + (hid0 + 2 * g + 3))
                for half in range(2):
                    if half == 0 or more:
                        split(nxt())
                    for q in range(4):
                        k = 4 * half + q
                        residual(k)
                        if gain is not None:
                            low_part(k, lo, gain, xcount + k + 1)
                        add_square(final_norm_, k, lo)

            for b in range(2):
                dve.sem_inc(c_free[b], 1)
            tile(0)
            nc.vector.tensor_copy(COL[:], SET[0][:, 0:NVEC]).then_inc(t_free[0], 1)
            dve.wait_ge(t_free[0], 1)
            tt(LBM[:], COL[:, LB0:LB0 + 8], COL[:, LB1:LB1 + 8], ALU.max).then_inc(lb_step, 1)
            dve.wait_ge(lb_step, 1)
            tt(LB[:], COL[:, LB0:LB0 + 8], LBM[:], ALU.subtract).then_inc(lb_step, 1)
            tt(OLB[:], COL[:, LB1:LB1 + 8], LBM[:], ALU.subtract).then_inc(lb_step, 1)
            dve.wait_ge(masks_loaded, 16)
            nc.vector.tensor_copy(masks[:], MS[:]).then_inc(pad_set, 1)
            tile(1)
            nc.vector.tensor_copy(CWT[:].rearrange("p i t -> p (i t)"), SET[1][:, 0:4 * TAPS]).then_inc(t_free[1], 1)
            dve.wait_ge(lb_exp, 2)
            tt(LBM[:], LB[:], OLB[:], ALU.add).then_inc(lb_step, 1)
            dve.wait_ge(lb_step, 4)
            nc.vector.reciprocal(LBM[:], LBM[:]).then_inc(lb_step, 1)
            dve.wait_ge(lb_step, 5)
            tt(LB[:], LB[:], LBM[:], ALU.mult).then_inc(lb_step, 1)
            tt(OLB[:], OLB[:], LBM[:], ALU.mult).then_inc(lb_step, 1)
            for t in range(-1, NCH):
                s = (t + 1) % 2
                if s == 1:
                    tiles[s].add()
                    continue
                tile(s)
                n, a = (META, 0) if t < 0 else (P, META + t * P)
                nc.vector.tensor_copy(H[:, :, a:a + n], SET[s][:, 0:KD * n].rearrange("p (k n) -> p k n", k=KD)).then_inc(t_free[s], 1)
            split(FFN1_S0)
            for k in range(KD):
                low_part(k, 0, G_FFN1, k + 1)
                add_square(0, k, 0)
            ffn(0, FFN1_S0, 0, 0, 1, G_MIX, KD, True)

            dve.wait_ge(h_saved, 16 * KD)
            nc.vector.memset(GLU[:, META + PROMPT:GLU_S], 0.0)
            nc.vector.memset(GLU[:, GLU_S + META + SAMPLE:GLU_LEN], 0.0).then_inc(pad_set, 1)

            def blocks_of(buf, lo, h):
                return buf[:, lo:T].rearrange("p (n two h) -> p n two h", two=2, h=h)

            def decays(l, direction):
                h = 1 << l
                nf, nb = (T if h <= META else DATA) // h, DATA // h
                if l == 0:
                    return FF[:, 0:T] if direction == 0 else FB[:, META:T]
                if l == 7:
                    return FL[:, direction, :]
                buf = KS if l % 2 else FF
                return buf[:, 0:nf] if direction == 0 else buf[:, nf:nf + nb]

            def raise_level(l):
                h = 1 << l
                for d, (A, B) in enumerate(((AF, BF), (AB, BB))):
                    F = decays(l, d)
                    with_meta = d == 0 and 2 * h <= META
                    if d == 0 and h == META:
                        F = F[:, 1:]
                    pairs = F.rearrange("p (n two) -> p n two", two=2)
                    skip = META // (2 * h) if with_meta else 0
                    far, near = (1, 0) if d == 0 else (0, 1)

                    def spread(half, a):
                        v = pairs[:, a:, half:half + 1]
                        return v.broadcast_to([P, v.shape[1], h]) if h > 1 else v

                    a = blocks_of(A, 0 if with_meta else META, h)[:, :, near, :]
                    tt(a, a, spread(far, 0), ALU.mult)
                    b = blocks_of(B, META, h)[:, :, far, :]
                    tt(b, b, spread(near, skip), ALU.mult)
                    up = tt(decays(l + 1, d), pairs[:, :, 0], pairs[:, :, 1], ALU.mult)
                return up

            def rec(stage, h):
                base = h * (PIECES // 2)

                def piece(name, n):
                    q = STAGE[name] + n
                    dve.wait_ge(c_full[q % 2], base + (q // 2 + 1))
                    return CB_[q % 2], c_free[q % 2], base + (q // 2 + 2)

                if stage == 0:
                    for ready in (q_ready, f_ready, fb_ready, kf_ready, kb_ready):
                        dve.wait_ge(ready, h + 1)
                    tt(BF[:, META:T], Q[:, META:T], FF[:, META:T], ALU.mult)
                    tt(BB[:, META:T], Q[:, META:T], FB[:, META:T], ALU.mult)
                    tt(KS[:, META:T], AF[:, META:T], AB[:, META:T], ALU.add).then_inc(bks_ready, 1)
                    dve.wait_ge(sc_free, h + 1)
                    for n, (c0, c1) in enumerate(CHUNK_PIECES):
                        bank, free, _ = piece("diag", n)
                        three = lambda v: v.rearrange("p (c t) -> p c t", t=P)
                        tt(three(SC[:, META + c0 * P:META + c1 * P]), three(bank[:, 0:(c1 - c0) * P]),
                           ident[:].rearrange("p (c t) -> p c t", c=1).broadcast_to([P, c1 - c0, P]),
                           ALU.mult).then_inc(free, 1)
                if stage < len(LEVELS):
                    for n, (c0, c1) in enumerate(CHUNK_PIECES):
                        bank, free, _ = piece(LEVELS[stage], n)
                        dve.sem_inc(dve_passed, 1)
                        three = lambda v: v.rearrange("p (c t) -> p c t", t=P)
                        nc.vector.copy_predicated(three(SC[:, META + c0 * P:META + c1 * P]),
                                                  masks[:, stage:stage + 1, :].broadcast_to([P, c1 - c0, P]),
                                                  three(bank[:, 0:(c1 - c0) * P])).then_inc(free, 1)
                    if stage:
                        dve.wait_ge(level_up, 7 * h + stage)
                    else:
                        dve.wait_ge(bks_ready, h + 1)
                    raise_level(stage).then_inc(level_up, 1)
                if stage == 8:
                    prev = (level_up, 7 * h + 7)
                    steps = 0
                    for n, gs in enumerate(G_PIECES):
                        bank, free, freed = piece("g", n)
                        for j, (d, c) in enumerate(gs):
                            g = bank[:, j * P:(j + 1) * P]
                            last = j == len(gs) - 1
                            dve.wait_ge(*prev)
                            if c == "meta" or (d, c) in (("b", PCH - 1), ("b", NCH - 1)):
                                dst = KS[:, 0:P] if d == "f" else AF[:, (c - 1) * P:c * P]
                                ins = nc.vector.tensor_copy(dst, g)
                            elif d == "f":
                                ins = stt(KS[:, (c + 1) * P:(c + 2) * P], KS[:, state_f(c) * P:(state_f(c) + 1) * P],
                                          FL[:, 0, c:c + 1], g, ALU.mult, ALU.add)
                            else:
                                ins = stt(AF[:, (c - 1) * P:c * P], AF[:, c * P:(c + 1) * P], FL[:, 1, c:c + 1], g,
                                          ALU.mult, ALU.add)
                            if last:
                                ins.then_inc(free, 1)
                                prev = (free, freed)
                            else:
                                ins.then_inc(state_step, 1)
                                steps += 1
                                prev = (state_step, h * (len(ALL_G) - len(G_PIECES)) + steps)
                if stage == 10:
                    for n, (a, b) in enumerate(COL_PIECES):
                        bank, free, _ = piece("ss", n)
                        ts(KS[:, META + a:META + b], bank[:, 0:b - a], 1.0 / P, RMS_EPS, ALU.mult, ALU.add).then_inc(free, 1)
                if stage == 11:
                    dve.wait_ge(orms_ready, h + 1)
                    nc.vector.reciprocal(KS[:, META:T], KS[:, META:T]).then_inc(ors_ready, 1)
                    dve.wait_ge(ors_ready, h + 1)
                    hgn = COL[:, HGN + h:HGN + h + 1] if isinstance(h, int) else COL[:, bass.ds(h + HGN, 1)]
                    stt(AB[:, META:T], AB[:, META:T], hgn, KS[:, META:T], ALU.mult, ALU.mult).then_inc(yn_ready, 1)
                    dve.wait_ge(yn_ready, h + 1)
                    tt(SC[:, META:T], AB[:, META:T], GS[:, META:T], ALU.mult).then_inc(y_ready, 1)

            def taps(i, first, count):
                col = lambda v, c: v[:, c:c + 1]
                for j in range(first, first + count):
                    src = GLU[:, 1 + j:1 + j + COUT_LEN]
                    w = (CWT[:, i, j:j + 1] if isinstance(i, int) else
                         CWT[:, bass.ds(i, 1), j:j + 1].rearrange("p a t -> p (a t)"))
                    if j == 0:
                        dve.wait_ge(glu_ready, i + 1)
                        dve.wait_ge(c_saved, i * 32)
                        cb = COL[:, CB + i:CB + i + 1] if isinstance(i, int) else COL[:, bass.ds(i + CB, 1)]
                        ts(COUT[:, 0:COUT_LEN], src, w, cb, ALU.mult, ALU.add).then_inc(tap_done, 1)
                    else:
                        dve.wait_ge(tap_done, i * (TAPS - 1) + j)
                        stt(COUT[:, 0:COUT_LEN], src, w, COUT[:, 0:COUT_LEN], ALU.mult, ALU.add)\
                            .then_inc(conv_ready if j == TAPS - 1 else tap_done, 1)

            TAP_SLOTS = {4: 4, 5: 3, 6: 3, 7: 3, 8: 3, 9: 3, 10: 3, 11: 3, 12: 3, 13: 3}

            def evacuate(i, pos):
                s = pos % 2
                lo = META if pos in (3, 5, 6) else 0
                tile(s)
                if pos == 5:
                    dve.wait_ge(kf_raw, i + 1)
                if pos == 6:
                    dve.wait_ge(kb_raw, i + 1)
                out = T2 if pos == 1 else VT if pos == 2 else T1
                tt(out[:, lo:T], SET[s][:, 0:T - lo], R[:, lo:T], ALU.mult).then_inc(t_free[s], 1)
                if pos == 1:
                    dve.wait_ge(glu_sig, i + 1)
                    tt(GLU[:, 0:META + PROMPT], T1[:, 0:META + PROMPT], T2[:, 0:META + PROMPT], ALU.mult)
                    tt(GLU[:, GLU_S:GLU_S + META], T1[:, 0:META], T2[:, 0:META], ALU.mult)
                    tt(GLU[:, GLU_S + META:GLU_S + META + SAMPLE], T1[:, META + PROMPT:T], T2[:, META + PROMPT:T],
                       ALU.mult).then_inc(glu_ready, 1)
                if pos == 3:
                    dve.wait_ge(q_sig, i + 1)
                    tt(Q[:, lo:T], T1[:, lo:T], T2[:, lo:T], ALU.mult).then_inc(q_ready, 1)
                if pos in (4, 5):
                    sig, F, ready, ld = ((f_sig, FF, f_ready, 0), (fb_sig, FB, fb_ready, HEADS))[pos - 4]
                    dve.wait_ge(sig, i + 1)
                    olb, lb = ((v[:, i + ld:i + ld + 1] if isinstance(i, int) else v[:, bass.ds(i + ld, 1)])
                               for v in (OLB, LB))
                    ts(F[:, lo:T], T2[:, lo:T], olb, lb, ALU.mult, ALU.add).then_inc(ready, 1)
                if pos == 6:
                    dve.wait_ge(g_sig, i + 1)
                    tt(GS[:, lo:T], T1[:, lo:T], T2[:, lo:T], ALU.mult)

            def head(i, z, r):
                for slot in range(14):
                    pos = slot // 2
                    if r:
                        rec(slot, i - 1)
                    if z and slot % 2 == 0:
                        split((HEAD_SLOTS + HEAD_SLOTS[0:1])[pos + 1])
                    if z and slot in TAP_SLOTS:
                        taps(i, sum(TAP_SLOTS[a] for a in TAP_SLOTS if a < slot), TAP_SLOTS[slot])
                    if z and slot % 2:
                        if z == "first" and pos == 0:
                            inverse_rms(1, 1, 0)
                        evacuate(i, pos)

            dve.wait_ge(pad_set, 2)
            head(0, "first", False)
            with looped(dve, 1, HEADS, head_counts(uses, tiles)) as i:
                head(i, "z", True)
            head(HEADS, None, True)

            dve.wait_ge(c_back, 64)
            acc = T1[:, META:T]
            chunk = lambda n: CR[:, n, 0:DATA]
            tt(acc, chunk(0), chunk(1), ALU.add).then_inc(csum, 1)
            for n in (2, 3):
                dve.wait_ge(csum, n - 1)
                tt(acc, acc, chunk(n), ALU.add).then_inc(csum, 1)
            tile(1)
            for n in range(4):
                ins = stt(chunk(n), SET[1][:, 0:DATA], -1.0 / W, chunk(n), ALU.mult, ALU.add)
                ins.then_inc(cxc if n < 3 else t_free[1], 1)
            for n in range(1, 4):
                dve.wait_ge(csq, n + 1)
                if n > 1:
                    dve.wait_ge(cacc, n - 1)
                tt(T2[:, META:T], T2[:, META:T], T1[:, META:T], ALU.add).then_inc(cacc, 1)
            tile(0)
            ts(T1[:, META:T], SET[0][:, 0:DATA], 1.0 / W, LN_EPS, ALU.mult, ALU.add).then_inc(t_free[0], 1)
            dve.wait_ge(rms_ready, 3)
            nc.vector.reciprocal(T1[:, META:T], T1[:, META:T]).then_inc(r_ready, 1)
            dve.wait_ge(r_ready, 3)
            for n in range(4):
                tt(chunk(n), chunk(n), T1[:, META:T], ALU.mult).then_inc(cn, 1)
            for n in range(4):
                dve.wait_ge(csig, n + 1)
                ts(chunk(n), chunk(n), COL[:, LNG + n:LNG + n + 1], COL[:, LNB + n:LNB + n + 1],
                   ALU.mult, ALU.add).then_inc(caff, 1)
                dve.wait_ge(caff, n + 1)
                tt(chunk(n), chunk(n), T2[:, META:T], ALU.mult).then_inc(cact, 1)
                dve.wait_ge(xh_ready, 2 * KD + n + 1)
                tt(XL[:, 4 + n, META:T], chunk(n), XH[:, 4 + n, META:T].bitcast(F32), ALU.subtract).then_inc(xl_ready, 1)
            for n in range(HEADS):
                dve.wait_ge(xh_ready, 2 * KD + 4 + n + 1)
                tt(XL[:, n, META:T], (GLU, COUT)[n % 2][:, 0:DATA], XH[:, n, META:T].bitcast(F32), ALU.subtract)\
                    .then_inc(xl_ready, 1)
            dve.wait_ge(h_back, 16 * KD)
            for n in range(KD):
                split((OUT_SLOTS + [FFN2_S0])[n + 1])
                tile(n % 2)
                tt(H[:, n, META:T], SET[n % 2][:, 0:DATA], H[:, n, META:T], ALU.add).then_inc(t_free[n % 2], 1)
                add_square(2, n, META)
            for k in range(KD):
                low_part(k, META, G_FFN2, 3 * KD + k + 1)
            ffn(META, FFN2_S0, NF, 3, 3, None, 0, False)
            inverse_rms(4, 0, META)
            for k in range(KD):
                stt(H[:, k, META:T], H[:, k, META:T], COL[:, G_FIN + k:G_FIN + k + 1], R[:, META:T],
                    ALU.mult, ALU.mult).then_inc(fin_ready, 1)
            for t in range(1, NCH, 2):
                dve.wait_ge(t_full[0], tiles[0].now((t + 1) // 2))
                nc.vector.tensor_copy(XT[:, t, :], SET[0][:, 0:D]).then_inc(out_full[0], 1)


SBUF_BASE, SBUF_TOP = 16512, 229312


def level_masks():
    s, t = np.arange(P)[:, None], np.arange(P)[None, :]
    return np.stack([(s // (2 * h) == t // (2 * h)) & (s // h != t // h) for h in LEVELS], 1).astype(np.float32)


_INS = ["x_prompt", "x_sample", "meta_tokens", "ffn1_norm", "ffn1_w_gate", "ffn1_w_up", "ffn1_w_down", "mix_norm",
        "w_in", "lb_logits", "hg_norm", "conv_w", "conv_b", "conv_ln_g", "conv_ln_b", "w_out", "ffn2_norm",
        "ffn2_w_gate", "ffn2_w_up", "ffn2_w_down", "final_norm"]


def kernel(**inputs):
    import concourse.bacc as bacc
    from concourse.bass_utils import run_bass_kernel_spmd

    nc = bacc.Bacc("TRN2", target_bir_lowering=False, num_devices=1)
    arrays = {name: np.ascontiguousarray(inputs[name]) for name in _INS}
    arrays["identity"] = np.eye(P, dtype=np.float32)
    arrays["level_masks"] = level_masks()
    args = [nc.dram_tensor(f"in_{n}", a.shape, mybir.dt.from_np(a.dtype), kind="ExternalInput").ap()
            for n, a in arrays.items()]
    outs = [nc.dram_tensor(f"out_{n}", (1, rows, D), F32, kind="ExternalOutput").ap()
            for n, rows in (("prompt", PROMPT), ("sample", SAMPLE))]
    encoder(nc, *args, *outs)
    r = run_bass_kernel_spmd(nc, [{f"in_{n}": a for n, a in arrays.items()}], core_ids=[0])
    return tuple(r.results[0][f"out_{n}"] for n in ("prompt", "sample"))
```

```python
from contextlib import ExitStack, contextmanager

import numpy as np

import concourse.bass as bass
from concourse import mybir

F32 = mybir.dt.float32
F32R = mybir.dt.float32r
U8 = mybir.dt.uint8
ACT = mybir.ActivationFunctionType
ALU = mybir.AluOpType

P = 128
META = 16
PROMPT = 256
SAMPLE = 1024
T = META + PROMPT + SAMPLE
DATA = PROMPT + SAMPLE
D = 1024
KD = D // P
DFF = 2816
NF = DFF // P
GROUPS = NF // 2
W = 512
HEADS = 4
NCH = DATA // P
PCH = PROMPT // P
LEVELS = (1, 2, 4, 8, 16, 32, 64)
TAPS = 31
PAD = (TAPS - 1) // 2
RMS_EPS = 1e-6
LN_EPS = 1e-5
BUF = T * 4
GLU_LEN = META + PROMPT + PAD + META + SAMPLE + PAD
GLU_B = (GLU_LEN * 4 + 31) // 32 * 32
COUT_LEN = PROMPT + PAD + META + SAMPLE
GLU_S = META + PROMPT + PAD
RING = 3

G_FFN1, G_MIX, G_FFN2, G_FIN, LB0, LB1, HGN, CB, LNG, LNB, NVEC = 0, 8, 16, 24, 32, 40, 48, 52, 56, 60, 64

CHUNK_PIECES = [(0, 4), (4, 8), (8, 10)]
COL_PIECES = [(0, 512), (512, 1024), (1024, DATA)]
FWD_G = ["meta", 0] + list(range(PCH, NCH - 1))
BWD_G = [1] + list(range(NCH - 1, PCH, -1))
ALL_G = [("f", c) for c in FWD_G] + [("b", c) for c in BWD_G]
G_PIECES = [ALL_G[a:a + 4] for a in range(0, len(ALL_G), 4)]
TF_PIECES = [FWD_G[a:a + 4] for a in range(0, len(FWD_G), 4)]
TB_PIECES = [BWD_G[a:a + 4] for a in range(0, len(BWD_G), 4)]
V_ALL = ["meta"] + list(range(NCH))
V_PIECES = [V_ALL[a:a + 4] for a in range(0, len(V_ALL), 4)]
STAGE = {}
_at = 0
for _name, _n in ([("v", len(V_PIECES)), ("diag", 3)] + [(h, 3) for h in LEVELS]
                  + [("tf", len(TF_PIECES)), ("tb", len(TB_PIECES)), ("g", len(G_PIECES)), ("out", 3), ("ss", 1), ("rb", 3)]):
    STAGE[_name] = _at
    _at += _n
PIECES = _at
assert PIECES % 2 == 0
R_BANKS = (1, 0, 1)
REC_BASE = (3, 4)
PE_FIRST = 2
TAPS_BEFORE = {0: 2, 1: 2, 2: 1, 3: 2}
TAPS_NOW = {4: 2, 5: 2, 6: 2, 7: 4, 8: 2, 9: 4, 10: 2, 11: 2, 12: 2, 13: 2}
assert sum(TAPS_BEFORE.values()) + sum(TAPS_NOW.values()) == TAPS

EARLY = HEADS - 1
TAPS_LAST = {0: 2, 1: 3, 2: 2}
EARLY_OUT = {3: (7, 1), 4: (3, 1), 5: (4, 1), 6: (5, 1), 9: (0, 1), 10: (1, 1), 11: (2, 0), 12: (6, 1)}
EARLY_SLOTS = [0, 2, 1]
LATE = KD - EARLY


def state_f(c):
    return 0 if c == PCH else c


class Count:

    def __init__(self):
        self.fixed, self.i, self.per = 0, None, 0

    def now(self, more=0):
        return self.fixed + more if self.i is None else self.i * self.per + (self.fixed + more)

    def add(self, n=1):
        self.fixed += n


@contextmanager
def looped(eng, start, end, counts):
    at = [c.fixed for c, _ in counts]
    with eng.Fori(start, end) as i:
        for c, per in counts:
            c.i, c.per = i - start, per
        yield i
    for (c, per), a in zip(counts, at):
        assert c.fixed - a == per, (c.fixed - a, per)
        c.i = None
        c.fixed = a + per * (end - start)


def blocks(lo):
    return [(a, min(a + 512, T), a - lo) for a in range(lo, T, 512)]


def encoder(nc, x_prompt, x_sample, meta_tokens, ffn1_norm, ffn1_w_gate, ffn1_w_up, ffn1_w_down, mix_norm,
            w_in, lb_logits, hg_norm, conv_w, conv_b, conv_ln_g, conv_ln_b, w_out, ffn2_norm, ffn2_w_gate,
            ffn2_w_up, ffn2_w_down, final_norm, ident_d, masks_d, y_prompt, y_sample):
    ctx = ExitStack()
    with ctx:
        ctx.enter_context(nc.sbuf_tensor("arena", [P, (SBUF_TOP - SBUF_BASE) // 4 - 8], F32))
        place = [SBUF_BASE]

        def at(name, shape, dt, offset):
            return nc.alloc_sbuf_tensor_at(name, [P] + shape, dt, offset=offset)

        def take(nbytes):
            a = place[0]
            place[0] += (nbytes + 31) // 32 * 32
            assert place[0] <= SBUF_TOP, place[0]
            return a

        o_xh, o_xl = take(KD * BUF), take(KD * BUF)
        XH = at("XH", [KD, T], F32R, o_xh)
        XL = at("XL", [KD, T], F32R, o_xl)
        o_raw = take(RING * 4096)
        WR = at("WR", [RING, 1024], F32, o_raw)
        WH = at("WH", [RING, 1024], F32R, take(RING * 4096))
        o_wl = take(RING * 4096)
        WL = at("WL", [RING, 1024], F32R, o_wl)
        o_r = take(BUF)
        R = at("R", [T], F32, o_r)
        o_h = take(KD * BUF)
        H = at("H", [KD, T], F32, o_h)
        o_hid = take(4 * BUF + 2 * GLU_B)
        o_t1, o_t2 = take(BUF), take(BUF)
        HH = at("HH", [3, T], F32R, o_hid)
        HL = at("HL", [3, T], F32R, o_hid + 3 * BUF)
        T1, T2 = at("T1", [T], F32, o_t1), at("T2", [T], F32, o_t2)
        XT = at("XT", [NCH, D], F32, o_hid)
        XM = at("XM", [D], F32, o_r)
        STG = at("STG", [P], F32, o_xl)
        CWS = at("CWS", [W], F32, o_xl + 512)
        MS = at("MS", [len(LEVELS), P], F32, o_xl + 4096)
        Q, FF, FB, AF, AB, BF, BB, VT = (at(n, [T], F32, o_h + k * BUF)
                                         for k, n in enumerate(("Q", "FF", "FB", "AF", "AB", "BF", "BB", "VT")))
        MA, MB = FB, Q
        VTOK, GS, SC, KS = (at(n, [T], F32, o_hid + k * BUF) for k, n in enumerate(("VTOK", "GS", "SC", "KS")))
        GLU = at("GLU", [GLU_LEN], F32, o_hid + 4 * BUF)
        COUT = at("COUT", [GLU_LEN], F32, o_hid + 4 * BUF + GLU_B)
        YB = at("YB", [HEADS, T], F32, o_xl)
        CR = at("CR", [4, T], F32, o_xl + HEADS * BUF)
        CSQ = at("CSQ", [4, T], F32, o_xh + HEADS * BUF)
        SQ0 = at("SQ0", [NCH, D], F32, o_xh)
        SQM = at("SQM", [D], F32, o_wl)
        XO = at("XO", [NCH, D], F32, o_xh)
        small = {}
        for n, shape, dt, size in (("ident", [P], F32, 4), ("ones", [P], F32, 4), ("masks", [len(LEVELS), P], U8, 1),
                                   ("VM", [P], F32, 4), ("COL", [NVEC], F32, 4), ("CWT", [4, TAPS], F32, 4),
                                   ("LB", [8], F32, 4), ("OLB", [8], F32, 4), ("LBM", [8], F32, 4),
                                   ("FL", [2, NCH], F32, 4), ("RS", [NCH + 1], F32, 4), ("RH", [NCH], F32, 4)):
            small[n] = at(n, shape, dt, take(int(np.prod(shape)) * size))
        ident, ones, masks, VM, COL, CWT, LB, OLB, LBM, FL, RS, RH = (small[n] for n in (
            "ident", "ones", "masks", "VM", "COL", "CWT", "LB", "OLB", "LBM", "FL", "RS", "RH"))
        PS = ctx.enter_context(nc.psum_tensor("PS", [P, 4096], F32))
        SET = [PS[:, 0:1536], PS[:, 1536:3072]]
        CB_ = [PS[:, 3072:3584], PS[:, 3584:4096]]

        hsave = nc.dram_tensor("hsave", [KD, P, T], F32, kind="Internal").ap()
        ysave = nc.dram_tensor("ysave", [EARLY, P, DATA], F32, kind="Internal").ap()
        csave = nc.dram_tensor("csave", [EARLY, P, DATA], F32, kind="Internal").ap()

        def sem(name):
            return ctx.enter_context(nc.semaphore(name))

        raw_loaded = [sem(f"raw_loaded{s}") for s in range(RING)]
        split_hi = [sem(f"split_hi{s}") for s in range(RING)]
        split_lo = [sem(f"split_lo{s}") for s in range(RING)]
        t_full = [sem(f"t_full{s}") for s in range(2)]
        t_free = [sem(f"t_free{s}") for s in range(2)]
        c_full = [sem(f"c_full{s}") for s in range(2)]
        c_free = [sem(f"c_free{s}") for s in range(2)]
        x_loaded = [sem(f"x_loaded{t}") for t in range(NCH + 1)]
        ident_loaded, const_loaded, cw_loaded, masks_loaded = sem("ident_loaded"), sem("const_loaded"), sem("cw_loaded"), sem("masks_loaded")
        ones_set, lb_exp, lb_step, pad_set = (sem(n) for n in (
            "ones_set", "lb_exp", "lb_step", "pad_set"))
        sq_ready, acc_ready, xh_ready, xl_ready, rms_ready, r_ready = (sem(n) for n in (
            "sq_ready", "acc_ready", "xh_ready", "xl_ready", "rms_ready", "r_ready"))
        rows_ready, ms_ready, diag_ready = sem("rows_ready"), sem("ms_ready"), sem("diag_ready")
        hms_ready, hdiag_ready = sem("hms_ready"), sem("hdiag_ready")
        silu_ready, prod_ready, hid_hi, hid_lo = (sem(n) for n in ("silu_ready", "prod_ready", "hid_hi", "hid_lo"))
        h_saved, y_saved, c_saved, c_back, y_back = (sem(n) for n in ("h_saved", "y_saved", "c_saved", "c_back", "y_back"))
        h_back = [sem(f"h_back{n}") for n in range(KD)]
        (glu_sig, glu_ready, conv_ready, q_sig, q_ready, f_sig, kf_raw, kf_ready, f_ready, fb_sig, kb_raw, kb_ready,
         fb_ready, g_sig, bks_ready, osq_ready, orms_ready, ors_ready, y_ready) = (sem(n) for n in (
             "glu_sig", "glu_ready", "conv_ready", "q_sig", "q_ready", "f_sig", "kf_raw", "kf_ready", "f_ready",
             "fb_sig", "kb_raw", "kb_ready", "fb_ready", "g_sig", "bks_ready", "osq_ready", "orms_ready",
             "ors_ready", "y_ready"))
        sc_free = sem("sc_free")
        sp_passed, dve_passed, pool_passed = sem("sp_passed"), sem("dve_passed"), sem("pool_passed")
        level_up, tap_done, state_step = sem("level_up"), sem("tap_done"), sem("state_step")
        merged = sem("merged")
        conv_taken, cxc, csq, cn, cact = (sem(n) for n in ("conv_taken", "cxc", "csq", "cn", "cact"))
        csq_added, cdiag_ready, cms_ready, croot_ready, cinv_ready = (sem(n) for n in (
            "csq_added", "cdiag_ready", "cms_ready", "croot_ready", "cinv_ready"))
        fin_ready, out_stored = sem("fin_ready"), sem("out_stored")
        xo_ready = [sem("xo_ready0"), sem("xo_ready1")]

        block = ctx.enter_context(nc.Block())
        TOKEN_TILES = list(range(NCH)) + [-1]

        HEAD_SLOTS = [0, 1, 2, 0, 1, 2, 1]
        FFN_UNITS = 6 * GROUPS
        OUT_SLOTS = [n % RING for n in range(KD)]
        RESIDUAL = {n: H[:, n, META:T] for n in (0, 1, 2, 6, 7)}
        RESIDUAL.update({3: R[:, META:T], 4: GLU[:, 0:DATA], 5: COUT[:, 0:DATA]})
        FFN1_S0, FFN2_S0 = 0, KD % RING

        def ffn_counts(uses, tiles=None):
            return [(u, 4) for u in uses] + [(t, 12) for t in tiles or []]

        def head_counts(uses, tiles=None):
            return ([(u, HEAD_SLOTS.count(s)) for s, u in enumerate(uses)]
                    + [(t, 4 - s) for s, t in enumerate(tiles or [])])

        @block.sync
        def _(sp):
            sp.dma_start(ident[:], ident_d).then_inc(ident_loaded, 16)
            for t in range(NCH):
                src = x_prompt[0, t * P:(t + 1) * P, :] if t < PCH else x_sample[0, (t - PCH) * P:(t - PCH + 1) * P, :]
                sp.dma_start(XT[:, t, :], src).then_inc(x_loaded[t], 16)
            uses = [Count() for _ in range(RING)]

            def load(s, src, dst):
                sp.wait_ge(split_hi[s], uses[s].now())
                sp.wait_ge(split_lo[s], uses[s].now())
                sp.sem_inc(sp_passed, 1)
                sp.dma_start(dst(WR[:, s, :]), src).then_inc(raw_loaded[s], 16)
                uses[s].add()

            cols = lambda w: w[0].rearrange("(k p) n -> p k n", p=P)
            by_k = lambda v: v.rearrange("p (k n) -> p k n", k=KD)

            def ffn(w_gate, w_up, w_down, s0):
                n = [s0]

                def nxt():
                    n[0] += 1
                    return (n[0] - 1) % RING

                def gate_up(m):
                    for w in (w_gate, w_up):
                        load(nxt(), cols(w)[:, :, bass.ds(m * P, P)], by_k)

                def down(j):
                    rows = w_down[0].rearrange("(g c p) n -> g p c n", c=2, p=P)
                    for half in range(2):
                        src = rows[bass.ds(j, 1), :, :, half * 512:(half + 1) * 512].rearrange("g p c n -> (g p) c n")
                        load(nxt(), src, lambda v: v.rearrange("p (c n) -> p c n", c=2))

                def group(j):
                    gate_up(2 * j)
                    down(j - 1)
                    gate_up(2 * j + 1)

                gate_up(0)
                gate_up(1)
                with looped(sp, 0, (GROUPS - 1) // 2, ffn_counts(uses)) as t:
                    group(2 * t + 1)
                    group(2 * t + 2)
                down(GROUPS - 1)

            ffn(ffn1_w_gate, ffn1_w_up, ffn1_w_down, FFN1_S0)

            def head_units(i):
                for s, c in zip(HEAD_SLOTS, (5, 6, 3, 0, 1, 2, 4)):
                    load(s, cols(w_in)[:, :, bass.ds(i * P + c * W, P)], by_k)

            with looped(sp, 0, HEADS, head_counts(uses)) as i:
                head_units(i)
            for k in range(EARLY):
                load(EARLY_SLOTS[k], w_out[0][k * P:(k + 1) * P, :], lambda v: v)
            for n in range(KD):
                load(OUT_SLOTS[n], cols(w_out)[:, EARLY:KD, n * P:(n + 1) * P],
                     lambda v: v[:, 0:LATE * P].rearrange("p (k n) -> p k n", k=LATE))
            ffn(ffn2_w_gate, ffn2_w_up, ffn2_w_down, FFN2_S0)
            for t in range(NCH):
                sp.wait_ge(xo_ready[t % 2], t // 2 + 1)
                dst = y_prompt[0, t * P:(t + 1) * P, :] if t < PCH else y_sample[0, (t - PCH) * P:(t - PCH + 1) * P, :]
                sp.dma_start(dst, XO[:, t, :]).then_inc(out_stored, 16)
            sp.wait_ge(out_stored, 16 * NCH)

        @block.gpsimd
        def _(pool):
            pool.memset(ones[:], 1.0).then_inc(ones_set, 1)
            pool.sem_inc(sc_free, 1)
            pool.dma_start(XM[0:META, :], meta_tokens).then_inc(x_loaded[NCH], 16)
            for row, src in ((G_FFN1, ffn1_norm), (G_MIX, mix_norm), (G_FFN2, ffn2_norm),
                             (HGN, hg_norm), (CB, conv_b), (LNG, conv_ln_g), (LNB, conv_ln_b)):
                n = src.shape[1] // P
                pool.dma_start(STG[row:row + n, :], src.rearrange("a (k p) -> (a k) p", p=P)).then_inc(const_loaded, 16)
            pool.dma_start(STG[G_FIN:G_FIN + KD, :], final_norm.rearrange("(k p) -> k p", p=P)).then_inc(const_loaded, 16)
            pool.dma_start(STG[LB0:LB0 + 16, :], lb_logits.rearrange("l d (h p) -> (l d h) p", p=P)).then_inc(const_loaded, 16)
            pool.dma_start(CWS[0:TAPS, :], conv_w[0]).then_inc(cw_loaded, 16)
            pool.dma_start(MS[:], masks_d).then_inc(masks_loaded, 16)
            for k in range(KD):
                pool.wait_ge(sq_ready, k + 1)
                pool.dma_start(hsave[k], H[:, k, :]).then_inc(h_saved, 16)

            def save_c(i):
                pool.wait_ge(conv_ready, i + 1)
                pool.sem_inc(pool_passed, 1)
                pool.dma_start(csave[bass.ds(i, 1), :, 0:PROMPT].rearrange("a p n -> (a p) n"),
                               COUT[:, 0:PROMPT]).then_inc(c_saved, 16)
                pool.dma_start(csave[bass.ds(i, 1), :, PROMPT:DATA].rearrange("a p n -> (a p) n"),
                               COUT[:, COUT_LEN - SAMPLE:COUT_LEN]).then_inc(c_saved, 16)

            def save_y(i):
                pool.wait_ge(y_ready, i + 1)
                pool.sem_inc(pool_passed, 1)
                pool.dma_start(ysave[bass.ds(i, 1), :, :].rearrange("a p n -> (a p) n"),
                               SC[:, META:T]).then_inc(y_saved, 16)
                pool.wait_ge(y_saved, 16 * (i + 1))
                pool.sem_inc(sc_free, 1)

            with pool.Fori(0, EARLY) as i:
                save_c(i)
                save_y(i)
            pool.wait_ge(g_sig, HEADS)
            pool.wait_ge(c_saved, 32 * EARLY)
            for n in range(EARLY):
                pool.dma_start(YB[:, n, META:T], ysave[n]).then_inc(y_back, 16)
            for n in range(EARLY):
                pool.dma_start(CR[:, n, META:T], csave[n]).then_inc(c_back, 16)

            def residual_back(n):
                pool.dma_start(RESIDUAL[n], hsave[n][:, META:T]).then_inc(h_back[n], 16)

            residual_back(3)
            pool.wait_ge(level_up, 7 * EARLY + 1)
            residual_back(7)
            pool.wait_ge(conv_taken, 1)
            residual_back(4)
            residual_back(5)
            pool.wait_ge(cms_ready, 1)
            residual_back(0)
            pool.wait_ge(osq_ready, HEADS)
            for n in (1, 2, 6):
                residual_back(n)

        @block.tensor
        def _(pe):
            uses = [Count() for _ in range(RING)]
            tiles = [Count(), Count()]

            def claim(s):
                pe.wait_ge(t_free[s], tiles[s].now())
                tiles[s].add()

            def unit(s):
                pe.wait_ge(split_lo[s], uses[s].now(1))
                uses[s].add()

            def product(s, wat, xh, xl, cols, first, last):
                for wt, xs in ((WH, (xh, xl)), (WL, (xh,))):
                    for x in xs:
                        for a, b, o in cols:
                            mm = nc.tensor.matmul(SET[s][:, o:o + b - a], wt[:, wat[0], wat[1]:wat[1] + P], x(a, b),
                                                  start=first and wt is WH and x is xh, stop=last and wt is WL)
                return mm

            def columns_in():
                for n, t in enumerate(TOKEN_TILES):
                    s = n % 2
                    pe.wait_ge(x_loaded[t if t >= 0 else NCH], 16)
                    claim(s)
                    for k in range(KD):
                        if t < 0:
                            mm = nc.tensor.transpose(SET[s][:, k * META:(k + 1) * META], XM[0:META, k * P:(k + 1) * P],
                                                     ident[0:META, 0:META])
                        else:
                            mm = nc.tensor.transpose(SET[s][:, k * P:(k + 1) * P], XT[:, t, k * P:(k + 1) * P], ident[:])
                    mm.then_inc(t_full[s], 1)

            pieces = [Count(), Count()]

            def small_piece(b):
                pe.wait_ge(c_free[b], pieces[b].now(1))
                pieces[b].add()
                return CB_[b]

            def row_sums(n, lo):
                pe.wait_ge(acc_ready, (KD - 1) * n)
                bank = small_piece(0)
                for c in ([] if lo else ["meta"]) + list(range(NCH)):
                    a, b = chunk_cols(c)
                    col = NCH if c == "meta" else c
                    mm = nc.tensor.matmul(bank[0:b - a, col:col + 1], T2[:, a:b], ones[:, 0:1], start=True, stop=True)
                mm.then_inc(c_full[0], 1)

            def spread_r(n, lo):
                pe.wait_ge(diag_ready, n + 1)
                for b, (c0, c1) in zip(R_BANKS, COL_PIECES):
                    bank = small_piece(b)
                    mm = nc.tensor.matmul(bank[:, 0:c1 - c0], ones[:], T1[:, META + c0:META + c1], start=True, stop=True)
                    if c1 == DATA and not lo:
                        mm = nc.tensor.matmul(bank[:, c1 - c0:c1 - c0 + META], ones[0:META, :], T1[0:META, 0:META],
                                              start=True, stop=True)
                    mm.then_inc(c_full[b], 1)

            def x_unit(slot, s, lo, norm=None, between=None):
                unit(slot)
                claim(s)
                for k in range(KD):
                    if norm is not None:
                        pe.wait_ge(xl_ready, KD * norm + k + 1)
                    if between is not None and k == 6:
                        spread_r(between, lo)
                    mm = product(s, (slot, k * P), lambda a, b: XH[:, k, a:b], lambda a, b: XL[:, k, a:b],
                                 blocks(lo), k == 0, k == KD - 1)
                mm.then_inc(t_full[s], 1)

            def chunk_cols(c):
                return (0, META) if c == "meta" else (META + c * P, META + (c + 1) * P)

            def leave(k, pieces_=(0, 1, 2)):
                pe.wait_ge(fin_ready, k + 1)
                for n in pieces_:
                    c0, c1 = CHUNK_PIECES[n]
                    b = (3 * k + n) % 2
                    bank = small_piece(b)
                    for c in range(c0, c1):
                        a, e = chunk_cols(c)
                        mm = nc.tensor.transpose(bank[:, (c - c0) * P:(c - c0 + 1) * P], H[:, k, a:e], ident[:])
                    mm.then_inc(c_full[b], 1)

            def ffn(lo, s0, xnorm, hid0):
                n = [s0]

                def nxt():
                    n[0] += 1
                    return (n[0] - 1) % RING

                def gate_up(norm=None):
                    r = None if norm is None else 0 if norm == 0 else 2
                    x_unit(nxt(), 0, lo, norm)
                    if r:
                        row_sums(r, lo)
                    x_unit(nxt(), 1, lo, between=r)

                def down(even, chunks, after=None, last=False):
                    def half_product(slot, q, c):
                        hs = (even, 2)[c]
                        return product(q % 2, (slot, c * 512 + q * P), lambda a, b: HH[:, hs, a:b],
                                       lambda a, b: HL[:, hs, a:b], blocks(lo), c == 0, c == 1)

                    pe.wait_ge(hid_lo, chunks - 1 if last else chunks)
                    for half in range(2):
                        slot = nxt()
                        unit(slot)
                        ahead = 2 if last and half == 0 else 0
                        for q in range(ahead):
                            claim(q % 2)
                            half_product(slot, q, 0)
                        if ahead:
                            pe.wait_ge(hid_lo, chunks)
                        for q in range(4):
                            s = q % 2
                            k = 4 * half + q
                            if q >= ahead:
                                claim(s)
                                half_product(slot, q, 0)
                            if after and k >= 3:
                                after(k - 3, (2,))
                            half_product(slot, q, 1).then_inc(t_full[s], 1)
                            if after and k >= 2:
                                after(k - 2, (0, 1))

                gate_up(xnorm)
                gate_up()
                with looped(pe, 0, (GROUPS - 1) // 2, ffn_counts(uses, tiles)) as t:
                    for g in range(2):
                        gate_up()
                        down(g, t * 4 + (hid0 + 2 * g + 2))
                        gate_up()
                down((GROUPS - 1) % 2, hid0 + NF, leave if hid0 else None, last=True)

            def rec(stage, h, chunks_between):
                base = h * (PIECES // 2)

                def piece(name, n):
                    q = STAGE[name] + n
                    pe.wait_ge(c_free[q % 2], base + (REC_BASE[q % 2] + q // 2 + 1))
                    return CB_[q % 2], c_full[q % 2]

                def before(name):
                    for q in (STAGE[name] - 2, STAGE[name] - 1):
                        pe.wait_ge(c_free[q % 2], base + (REC_BASE[q % 2] + q // 2 + 2))

                if stage == "v":
                    for n, cs in enumerate(V_PIECES):
                        if n == 2:
                            chunks_between(1)
                        bank, full = piece("v", n)
                        for j, c in enumerate(cs):
                            a, b = chunk_cols(c)
                            mm = nc.tensor.transpose(bank[0:b - a, j * P:(j + 1) * P], VT[:, a:b], ident[:])
                        mm.then_inc(full, 1)
                if stage == 0:
                    pe.wait_ge(bks_ready, h + 1)
                    for n, (c0, c1) in enumerate(CHUNK_PIECES):
                        bank, full = piece("diag", n)
                        for c in range(c0, c1):
                            a, b = chunk_cols(c)
                            mm = nc.tensor.matmul(bank[:, (c - c0) * P:(c - c0 + 1) * P], KS[:, a:b], Q[:, a:b],
                                                  start=True, stop=True)
                        mm.then_inc(full, 1)
                    chunks_between(1)
                if stage in range(len(LEVELS)):
                    hh = LEVELS[stage]
                    if stage:
                        pe.wait_ge(merged, (len(LEVELS) - 1) * h + stage)
                    for n, (c0, c1) in enumerate(CHUNK_PIECES):
                        if n == 2:
                            chunks_between(2 if stage else 1)
                        bank, full = piece(hh, n)
                        for c in range(c0, c1):
                            a, b = chunk_cols(c)
                            out = bank[:, (c - c0) * P:(c - c0 + 1) * P]
                            if stage:
                                mm = nc.tensor.matmul(out, MA[:, a:b], MB[:, a:b], start=True, stop=True)
                                continue
                            out = out.rearrange("p (n two h) -> p n two h", two=2, h=hh)
                            for A, B, half in ((AF, BF, 1), (AB, BB, 0)):
                                rhs = B[:, a:b].rearrange("p (n two h) -> p n two h", two=2, h=hh)
                                mm = nc.tensor.matmul(out[:, :, half, :], A[:, a:b], rhs[:, :, half, :],
                                                      start=True, stop=True)
                        mm.then_inc(full, 1)
                if stage == 7:
                    pe.wait_ge(level_up, 7 * h + 7)
                    for name, pieces, A in (("tf", TF_PIECES, AF), ("tb", TB_PIECES, AB)):
                        for n, cs in enumerate(pieces):
                            if (name, n) in (("tf", 2), ("tb", 1)):
                                chunks_between(1)
                            bank, full = piece(name, n)
                            for j, c in enumerate(cs):
                                a, b = chunk_cols(c)
                                mm = nc.tensor.transpose(bank[0:b - a, j * P:(j + 1) * P], A[:, a:b], ident[:])
                            mm.then_inc(full, 1)
                if stage == 8:
                    before("g")
                    for n, gs in enumerate(G_PIECES):
                        if n >= 2:
                            chunks_between(1)
                        bank, full = piece("g", n)
                        for j, (d, c) in enumerate(gs):
                            order = FWD_G if d == "f" else BWD_G
                            at_ = (FF if d == "f" else FB)[:, order.index(c) * P:(order.index(c) + 1) * P]
                            if c == "meta":
                                mm = nc.tensor.matmul(bank[:, j * P:(j + 1) * P], at_[0:META, :], VM[0:META, :],
                                                      start=True, stop=True)
                            else:
                                mm = nc.tensor.matmul(bank[:, j * P:(j + 1) * P], at_, VTOK[:, c * P:(c + 1) * P],
                                                      start=True, stop=True)
                        mm.then_inc(full, 1)
                if stage == 9:
                    before("out")
                    for n, (c0, c1) in enumerate(CHUNK_PIECES):
                        if n == 2:
                            chunks_between(1)
                        bank, full = piece("out", n)
                        for c in range(c0, c1):
                            a, b = chunk_cols(c)
                            out = bank[:, (c - c0) * P:(c - c0 + 1) * P]
                            last = c in (PCH - 1, NCH - 1)
                            nc.tensor.matmul(out, VTOK[:, c * P:(c + 1) * P], SC[:, a:b], start=True, stop=False)
                            mm = nc.tensor.matmul(out, KS[:, state_f(c) * P:(state_f(c) + 1) * P], BF[:, a:b],
                                                  start=False, stop=last)
                            if not last:
                                mm = nc.tensor.matmul(out, AF[:, c * P:(c + 1) * P], BB[:, a:b], start=False, stop=True)
                        mm.then_inc(full, 1)
                if stage == 10:
                    pe.wait_ge(osq_ready, h + 1)
                    bank, full = piece("ss", 0)
                    for c in range(NCH):
                        a, b = chunk_cols(c)
                        mm = nc.tensor.matmul(bank[:, c:c + 1], SC[:, a:b], ones[:, 0:1], start=True, stop=True)
                    mm.then_inc(full, 1)
                if stage == 12:
                    pe.wait_ge(hdiag_ready, h + 1)
                    for n, (a, b) in enumerate(COL_PIECES):
                        if n == 2:
                            chunks_between(2)
                        bank, full = piece("rb", n)
                        nc.tensor.matmul(bank[:, 0:b - a], ones[:], KS[:, META + a:META + b],
                                         start=True, stop=True).then_inc(full, 1)

            pe.wait_ge(ident_loaded, 16)
            columns_in()
            pe.wait_ge(const_loaded, 16 * 9)
            claim(1)
            nc.tensor.transpose(SET[1][:, 0:NVEC], STG[0:NVEC, :], ident[0:NVEC, 0:NVEC]).then_inc(t_full[1], 1)
            pe.wait_ge(cw_loaded, 16)
            claim(0)
            for i in range(4):
                mm = nc.tensor.transpose(SET[0][:, i * TAPS:(i + 1) * TAPS], CWS[0:TAPS, i * P:(i + 1) * P],
                                         ident[0:TAPS, 0:TAPS])
            mm.then_inc(t_full[0], 1)
            pe.wait_ge(ones_set, 1)
            ffn(0, FFN1_S0, 0, 0)

            def head(i, z, r):
                for pos in range(7):
                    slot = HEAD_SLOTS[pos] if z else None
                    s = pos % 2
                    lo = META if pos in (3, 5, 6) else 0
                    first = z == "first" and pos == 0
                    if z:
                        unit(slot)
                    ends = [None]
                    for half in range(2):
                        left = [4 * half, 4 * half + 4]

                        def chunks_between(n):
                            if not z:
                                return
                            for k in range(left[0], min(left[0] + n, left[1])):
                                if first:
                                    pe.wait_ge(xl_ready, KD + k + 1)
                                if z == "first" and pos == 1 and k == 6:
                                    spread_r(1, 0)
                                ends[0] = product(s, (slot, k * P), lambda a, b: XH[:, k, a:b],
                                                  lambda a, b: XL[:, k, a:b], blocks(lo), k == 0, k == KD - 1)
                            left[0] = min(left[0] + n, left[1])

                        if z and half == 0:
                            claim(s)
                        if r:
                            chunks_between(PE_FIRST)
                            rec(2 * pos + half, i - 1, chunks_between)
                        if z and pos == 6 and half == 1:
                            chunks_between(2)
                            rec("v", i, chunks_between)
                        chunks_between(4)
                    if z:
                        ends[0].then_inc(t_full[s], 1)
                    if first:
                        row_sums(1, 0)

            head(0, "first", False)
            with looped(pe, 1, HEADS, head_counts(uses, tiles)) as i:
                head(i, "z", True)

            def channel_sums(ns):
                for n in ns:
                    for a, b in COL_PIECES:
                        mm = nc.tensor.matmul(SET[0][:, a:b], ones[:], CR[:, n, META + a:META + b], start=n == 0, stop=n == 3)
                return mm

            def square_sums():
                claim(0)
                for c in range(NCH):
                    a, b = chunk_cols(c)
                    mm = nc.tensor.matmul(SET[0][:, c:c + 1], CSQ[:, 0, a:b], ones[:, 0:1], start=True, stop=True)
                mm.then_inc(t_full[0], 1)

            def spread_c():
                claim(0)
                for a, b in COL_PIECES:
                    mm = nc.tensor.matmul(SET[0][:, a:b], ones[:], T1[:, META + a:META + b], start=True, stop=True)
                mm.then_inc(t_full[0], 1)

            for slot in range(14):
                out = EARLY_OUT.get(slot)
                left = [0, EARLY if out else 0]

                def chunks_between(n):
                    for k in range(left[0], min(left[0] + n, left[1])):
                        if k == 0:
                            claim(out[1])
                        if slot == min(EARLY_OUT):
                            unit(EARLY_SLOTS[k])
                            pe.wait_ge(xl_ready, 2 * KD + k + 1)
                        mm = product(out[1], (EARLY_SLOTS[k], out[0] * P), lambda a, b: XH[:, k, a:b],
                                     lambda a, b: XL[:, k, a:b], blocks(META), k == 0, k == EARLY - 1)
                        if k == EARLY - 1:
                            mm.then_inc(t_full[out[1]], 1)
                    left[0] = min(left[0] + n, left[1])

                rec(slot, HEADS - 1, chunks_between)
                chunks_between(EARLY)
                if slot == 2:
                    pe.wait_ge(c_back, 16 * EARLY)
                    claim(0)
                    channel_sums(range(EARLY))
                if slot == 4:
                    pe.wait_ge(conv_taken, 1)
                    channel_sums([EARLY]).then_inc(t_full[0], 1)
                if slot == 7:
                    pe.wait_ge(csq_added, 3)
                    square_sums()
                if slot == 8:
                    pe.wait_ge(cdiag_ready, 1)
                    spread_c()
            for b in range(2):
                pieces[b].add(HEADS * PIECES // 2)

            def out_chunks(n, ks):
                for k in ks:
                    mm = product(n % 2, (OUT_SLOTS[n], (k - EARLY) * P), lambda a, b: XH[:, k, a:b],
                                 lambda a, b: XL[:, k, a:b], blocks(META), k == HEADS, k == EARLY)
                if EARLY in ks:
                    mm.then_inc(t_full[n % 2], 1)

            conv_ks = range(HEADS, KD)
            pe.wait_ge(xl_ready, 3 * KD - 1)
            for n in range(2):
                unit(OUT_SLOTS[n])
                claim(n % 2)
                out_chunks(n, conv_ks)
            pe.wait_ge(xl_ready, 3 * KD)
            for n in range(2):
                out_chunks(n, [EARLY])
            for n in range(2, KD):
                unit(OUT_SLOTS[n])
                claim(n % 2)
                out_chunks(n, list(conv_ks) + [EARLY])
            ffn(META, FFN2_S0, 3, NF)
            leave(KD - 3, (2,))
            leave(KD - 2)
            leave(KD - 1)
            row_sums(3, META)

        @block.scalar
        def _(act):
            uses = [Count() for _ in range(RING)]
            tiles = [Count(), Count()]

            def split(s, settled=True, n=1024):
                act.wait_ge(raw_loaded[s], uses[s].now(1) * 16)
                if settled:
                    for b in range(2):
                        act.wait_ge(t_full[b], tiles[b].now())
                nc.scalar.activation(WH[:, s, 0:n], WR[:, s, 0:n], ACT.Copy).then_inc(split_hi[s], 1)
                uses[s].add()

            def roots(n, lo):
                act.wait_ge(ms_ready, n + 1)
                if not lo:
                    nc.scalar.activation(RS[0:META, NCH:NCH + 1], RS[0:META, NCH:NCH + 1], ACT.Sqrt)
                nc.scalar.activation(RS[:, 0:NCH], RS[:, 0:NCH], ACT.Sqrt).then_inc(rms_ready, 1)

            def gained(k, lo, gain):
                nc.scalar.activation(XH[:, k, lo:T], H[:, k, lo:T], ACT.Copy,
                                     scale=COL[:, gain + k:gain + k + 1]).then_inc(xh_ready, 1)

            def squared(n, k, lo):
                if k >= 2:
                    act.wait_ge(acc_ready, (KD - 1) * (n - 1) + k - 1)
                nc.scalar.activation((T1 if k else T2)[:, lo:T], H[:, k, lo:T], ACT.Square).then_inc(sq_ready, 1)

            pieces = [Count(), Count()]
            for b in range(2):
                pieces[b].add(REC_BASE[b] + HEADS * PIECES // 2 + 2)

            def leave(k):
                for n, (c0, c1) in enumerate(CHUNK_PIECES):
                    b = (3 * k + n) % 2
                    pieces[b].add()
                    act.wait_ge(c_full[b], pieces[b].now())
                    nc.scalar.activation(XO[:, c0:c1, k * P:(k + 1) * P],
                                         CB_[b][:, 0:(c1 - c0) * P].rearrange("p (c n) -> p c n", n=P),
                                         ACT.Copy).then_inc(c_free[b], 1)

            def ffn(lo, s0, hid0, final_norm_, gain, more):
                n = [s0 + 1]

                def nxt():
                    n[0] += 1
                    return (n[0] - 1) % RING

                def gate_up(hs, chunk, first=False):
                    split(nxt())
                    if first and final_norm_ == 3:
                        roots(2, lo)
                    tiles[0].add()
                    act.wait_ge(t_free[0], tiles[0].now())
                    nc.scalar.activation(T2[:, lo:T], T1[:, lo:T], ACT.Silu).then_inc(silu_ready, 1)
                    split(nxt())
                    tiles[1].add()
                    act.wait_ge(prod_ready, chunk + 1)
                    nc.scalar.activation(HH[:, hs, lo:T], T2[:, lo:T], ACT.Copy).then_inc(hid_hi, 1)

                gate_up(0, hid0, True)
                gate_up(2, hid0 + 1)
                with looped(act, 0, (GROUPS - 1) // 2, ffn_counts(uses, tiles)) as t:
                    for g in range(2):
                        gate_up(1 - g, t * 4 + (hid0 + 2 * g + 2))
                        for half in range(2):
                            split(nxt())
                            for b in range(2):
                                tiles[b].add(2)
                        gate_up(2, t * 4 + (hid0 + 2 * g + 3))
                for half in range(2):
                    if half == 0 or more:
                        split(nxt())
                    for q in range(4):
                        b, k = q % 2, 4 * half + q
                        tiles[b].add()
                        act.wait_ge(t_free[b], tiles[b].now())
                        if gain is not None:
                            gained(k, lo, gain)
                        squared(final_norm_, k, lo)
                        if not more and k >= 2:
                            leave(k - 2)

            for n, t in enumerate(TOKEN_TILES):
                act.wait_ge(x_loaded[t if t >= 0 else NCH], 16)
                if t < 0:
                    nc.scalar.activation(SQM[0:META, :], XM[0:META, :], ACT.Square,
                                         accum_out=RS[0:META, NCH:NCH + 1]).then_inc(rows_ready, 1)
                else:
                    nc.scalar.activation(SQ0[:, t, :], XT[:, t, :], ACT.Square, accum_out=RS[:, t:t + 1])
                s = n % 2
                tiles[s].add()
                if s == 1:
                    act.wait_ge(t_full[s], tiles[s].now())
                    nc.scalar.activation(H[:, :, META + t * P:META + (t + 1) * P],
                                         SET[s][:, 0:D].rearrange("p (k n) -> p k n", k=KD), ACT.Copy).then_inc(t_free[s], 1)
            tiles[0].add()
            tiles[1].add()
            split(FFN1_S0, settled=False)
            act.wait_ge(t_free[0], tiles[0].now())
            act.wait_ge(t_free[1], tiles[1].now())
            roots(0, 0)
            for k in range(KD):
                gained(k, 0, G_FFN1)
            act.wait_ge(lb_step, 3)
            nc.scalar.activation(LB[:], LB[:], ACT.Exp).then_inc(lb_exp, 1)
            nc.scalar.activation(OLB[:], OLB[:], ACT.Exp).then_inc(lb_exp, 1)
            ffn(0, FFN1_S0, 0, 1, G_MIX, True)

            def rec(stage, h):
                base = h * (PIECES // 2)

                def piece(name, n):
                    q = STAGE[name] + n
                    act.wait_ge(c_full[q % 2], base + (REC_BASE[q % 2] + q // 2 + 1))
                    return CB_[q % 2], c_free[q % 2]

                def read_out(name):
                    last = STAGE[name] + 2
                    for q in (last - 1, last):
                        act.wait_ge(c_free[q % 2], base + (REC_BASE[q % 2] + q // 2 + 2))

                if stage == "v":
                    for n, cs in enumerate(V_PIECES):
                        bank, free = piece("v", n)
                        if cs[0] == "meta":
                            nc.scalar.activation(VM[0:META, :], bank[0:META, 0:P], ACT.Copy)
                            cs, bank = cs[1:], bank[:, P:512]
                        nc.scalar.activation(VTOK[:, cs[0] * P:(cs[-1] + 1) * P], bank[:, 0:len(cs) * P],
                                             ACT.Copy).then_inc(free, 1)
                if stage in range(len(LEVELS) - 1):
                    act.wait_ge(level_up, 7 * h + (stage + 1))
                    if stage:
                        for n in (1, 2):
                            piece(LEVELS[stage], n)
                    hh = LEVELS[stage + 1]
                    for dst, src, half in ((MA, AF, 0), (MB, BB, 0), (MB, BF, 1), (MA, AB, 1)):
                        to, of = (v[:, META:T].rearrange("p (n two h) -> p n two h", two=2, h=hh)[:, :, half, :]
                                  for v in (dst, src))
                        ins = nc.scalar.activation(to, of, ACT.Copy)
                    ins.then_inc(merged, 1)
                if stage == 7:
                    for name, pieces, dst in (("tf", TF_PIECES, FF), ("tb", TB_PIECES, FB)):
                        for n, cs in enumerate(pieces):
                            bank, free = piece(name, n)
                            at0 = n * 4 * P
                            if cs[0] == "meta":
                                nc.scalar.activation(dst[0:META, 0:P], bank[0:META, 0:P], ACT.Copy)
                                cs, at0, bank = cs[1:], at0 + P, bank[:, P:512]
                            nc.scalar.activation(dst[:, at0:at0 + len(cs) * P], bank[:, 0:len(cs) * P],
                                                 ACT.Copy).then_inc(free, 1)
                if stage == 9:
                    for n, (c0, c1) in enumerate(CHUNK_PIECES):
                        bank, free = piece("out", n)
                        nc.scalar.activation(BF[:, META + c0 * P:META + c1 * P], bank[:, 0:(c1 - c0) * P],
                                             ACT.Copy).then_inc(free, 1)
                    read_out("out")
                    nc.scalar.activation(SC[:, META:T], BF[:, META:T], ACT.Square).then_inc(osq_ready, 1)
                if stage == 11:
                    act.wait_ge(hms_ready, h + 1)
                    nc.scalar.activation(RH[:], RH[:], ACT.Sqrt).then_inc(orms_ready, 1)

            def head(i, z, r):
                for pos in range(7):
                    s = pos % 2
                    if z:
                        split((HEAD_SLOTS + HEAD_SLOTS[0:1])[pos + 1])
                        tiles[s].add()
                    if r:
                        rec(2 * pos, i - 1)
                    if z == "first" and pos == 1:
                        roots(1, 0)
                    if r:
                        rec(2 * pos + 1, i - 1)
                    if not z:
                        continue
                    if pos == 6:
                        rec("v", i)
                    if pos in (1, 3, 4, 5, 6):
                        act.wait_ge(t_free[s], tiles[s].now())
                    if pos == 1:
                        nc.scalar.activation(T2[:], T2[:], ACT.Sigmoid).then_inc(glu_sig, 1)
                    if pos == 3:
                        nc.scalar.activation(T2[:, META:T], T1[:, META:T], ACT.Sigmoid).then_inc(q_sig, 1)
                    if pos == 4:
                        forget(i, 0, AF, f_sig, kf_raw, kf_ready, 0)
                    if pos == 5:
                        forget(i, META, AB, fb_sig, kb_raw, kb_ready, HEADS)
                    if pos == 6:
                        nc.scalar.activation(T2[:, META:T], T1[:, META:T], ACT.Sigmoid).then_inc(g_sig, 1)

            def forget(i, lo, A, sig, raw, ready, ld):
                nc.scalar.activation(T2[:, lo:T], T1[:, lo:T], ACT.Sigmoid).then_inc(sig, 1)
                nc.scalar.activation(A[:, lo:T], T1[:, lo:T], ACT.Sigmoid, scale=-1.0).then_inc(raw, 1)
                act.wait_ge(raw, i + 1)
                olb = OLB[:, i + ld:i + ld + 1] if isinstance(i, int) else OLB[:, bass.ds(i + ld, 1)]
                nc.scalar.activation(A[:, lo:T], A[:, lo:T], ACT.Copy, scale=olb).then_inc(ready, 1)

            act.wait_ge(h_saved, 16 * KD)
            head(0, "first", False)
            with looped(act, 1, HEADS, head_counts(uses, tiles)) as i:
                head(i, "z", True)

            def hi_part(n, src):
                nc.scalar.activation(XH[:, n, META:T], src, ACT.Copy).then_inc(xh_ready, 1)

            def swish(n):
                if n < 3:
                    act.wait_ge(cn, n + 1)
                else:
                    act.wait_ge(t_free[0], tiles[0].now())
                nc.scalar.activation(CR[:, n, META:T], CR[:, n, META:T], ACT.Silu, scale=COL[:, LNG + n:LNG + n + 1],
                                     bias=COL[:, LNB + n:LNB + n + 1]).then_inc(cact, 1)
                act.wait_ge(cact, n + 1)
                hi_part(HEADS + n, CR[:, n, META:T])

            for slot in range(14):
                if slot == 0:
                    for k in range(1, EARLY):
                        split(EARLY_SLOTS[k])
                    act.wait_ge(y_back, 16 * EARLY)
                    for n in range(EARLY):
                        hi_part(n, YB[:, n, META:T])
                if slot == 9:
                    swish(0)
                    swish(1)
                rec(slot, HEADS - 1)
                if slot in EARLY_OUT:
                    tiles[EARLY_OUT[slot][1]].add()
                if slot == 3:
                    act.wait_ge(conv_ready, HEADS)
                    nc.scalar.activation(CR[:, 3, META:META + PROMPT], COUT[:, 0:PROMPT], ACT.Copy)
                    nc.scalar.activation(CR[:, 3, META + PROMPT:T], COUT[:, COUT_LEN - SAMPLE:COUT_LEN],
                                         ACT.Copy).then_inc(conv_taken, 1)
                if slot in (4, 7, 8):
                    tiles[0].add()
                if slot in (4, 5):
                    for n in ((0, 1), (2, 3))[slot - 4]:
                        if n < 3:
                            act.wait_ge(cxc, n + 1)
                        else:
                            act.wait_ge(t_free[0], tiles[0].now())
                        nc.scalar.activation(CSQ[:, n, META:T], CR[:, n, META:T], ACT.Square).then_inc(csq, 1)
                if slot == 7:
                    act.wait_ge(cms_ready, 1)
                    nc.scalar.activation(RS[:, 0:NCH], RS[:, 0:NCH], ACT.Sqrt).then_inc(croot_ready, 1)
                if slot == 9:
                    swish(2)
                    swish(3)
            for n in range(2):
                split(OUT_SLOTS[n], n=LATE * P)
            act.wait_ge(y_ready, HEADS)
            hi_part(EARLY, YB[:, EARLY, META:T])
            for n in range(KD):
                if n + 2 < KD:
                    split(OUT_SLOTS[n + 2], n=LATE * P)
                elif n + 2 == KD:
                    split(FFN2_S0)
                tiles[n % 2].add()
                act.wait_ge(t_free[n % 2], tiles[n % 2].now())
                if n < KD - 1:
                    squared(2, n, META)
            for k in range(KD):
                gained(k, META, G_FFN2)
                if k == 1:
                    squared(2, KD - 1, META)
            ffn(META, FFN2_S0, NF, 3, None, False)
            leave(KD - 2)
            leave(KD - 1)
            roots(3, META)
            for t in range(1, NCH, 2):
                if t == 1:
                    act.wait_ge(r_ready, 4)
                    for b in range(2):
                        act.wait_ge(c_free[b], pieces[b].now(1))
                nc.scalar.activation(XO[:, t, :], XO[:, t, :], ACT.Copy, scale=RS[:, t:t + 1]).then_inc(xo_ready[1], 1)

        @block.vector
        def _(dve):
            uses = [Count() for _ in range(RING)]
            tiles = [Count(), Count()]
            tt, stt, ts = nc.vector.tensor_tensor, nc.vector.scalar_tensor_tensor, nc.vector.tensor_scalar

            def split(s, n=1024):
                uses[s].add()
                dve.wait_ge(split_hi[s], uses[s].now())
                tt(WL[:, s, 0:n], WR[:, s, 0:n], WH[:, s, 0:n].bitcast(F32), ALU.subtract).then_inc(split_lo[s], 1)

            def tile(s):
                tiles[s].add()
                dve.wait_ge(t_full[s], tiles[s].now())

            pieces = [Count(), Count()]

            def small_piece(b):
                pieces[b].add()
                dve.wait_ge(c_full[b], pieces[b].now())
                return CB_[b]

            def mean_squares(n, lo):
                if n:
                    src = small_piece(0)
                else:
                    dve.wait_ge(rows_ready, 1)
                    src = RS
                if not lo:
                    meta = (slice(0, META), slice(NCH, NCH + 1))
                    ts(RS[meta], src[meta], 1.0 / D, RMS_EPS, ALU.mult, ALU.add)
                last = ts(RS[:, 0:NCH], src[:, 0:NCH], 1.0 / D, RMS_EPS, ALU.mult, ALU.add)
                if n:
                    last.then_inc(c_free[0], 1)
                    dve.wait_ge(c_free[0], pieces[0].now(1))
                    dve.sem_inc(ms_ready, 1)
                else:
                    last.then_inc(ms_ready, 1)

            def inverse(n, lo):
                dve.wait_ge(rms_ready, n + 1)
                if not lo:
                    nc.vector.reciprocal(RS[0:META, NCH:NCH + 1], RS[0:META, NCH:NCH + 1])
                nc.vector.reciprocal(RS[:, 0:NCH], RS[:, 0:NCH]).then_inc(r_ready, 1)
                dve.wait_ge(r_ready, n + 1)

            def diagonals(dst, r, ready):
                three = [P, NCH, P]
                tt(dst[:, META:T].rearrange("p (c t) -> p c t", t=P),
                   ident[:].rearrange("p (c t) -> p c t", c=1).broadcast_to(three),
                   r.rearrange("p (c t) -> p c t", t=1).broadcast_to(three), ALU.mult).then_inc(ready, 1)

            def make_r(n, lo):
                inverse(n, lo)
                if not lo:
                    ts(T1[0:META, 0:META], ident[0:META, 0:META], RS[0:META, NCH:NCH + 1], None, ALU.mult)
                diagonals(T1, RS[:, 0:NCH], diag_ready)
                for b, (c0, c1) in zip(R_BANKS, COL_PIECES):
                    bank = small_piece(b)
                    if c1 == DATA and not lo:
                        nc.vector.tensor_copy(R[:, 0:META], bank[:, c1 - c0:c1 - c0 + META])
                    nc.vector.tensor_copy(R[:, META + c0:META + c1], bank[:, 0:c1 - c0]).then_inc(c_free[b], 1)
                dve.wait_ge(c_free[R_BANKS[-1]], pieces[R_BANKS[-1]].now(1))

            def low_part(k, lo, gain, count):
                dve.wait_ge(xh_ready, count)
                stt(XL[:, k, lo:T], H[:, k, lo:T], COL[:, gain + k:gain + k + 1], XH[:, k, lo:T].bitcast(F32),
                    ALU.mult, ALU.subtract).then_inc(xl_ready, 1)

            def add_square(n, k, lo):
                if k:
                    dve.wait_ge(sq_ready, KD * (n - 1) + k + 1)
                    if k >= 2:
                        dve.wait_ge(acc_ready, (KD - 1) * (n - 1) + k - 1)
                    tt(T2[:, lo:T], T2[:, lo:T], T1[:, lo:T], ALU.add).then_inc(acc_ready, 1)

            def ffn(lo, s0, hid0, norm, final_norm_, gain, xcount, more):
                n = [s0 + 1]
                cols = T - lo

                def nxt():
                    n[0] += 1
                    return (n[0] - 1) % RING

                def hidden_lo(hs, chunk):
                    dve.wait_ge(hid_hi, chunk + 1)
                    tt(HL[:, hs, lo:T], T2[:, lo:T], HH[:, hs, lo:T].bitcast(F32), ALU.subtract).then_inc(hid_lo, 1)

                def gate_up(hs, chunk, first=False, lo_now=True):
                    split(nxt())
                    if first:
                        if norm:
                            mean_squares(norm, lo)
                        make_r(norm, lo)
                    tile(0)
                    tt(T1[:, lo:T], SET[0][:, 0:cols], R[:, lo:T], ALU.mult).then_inc(t_free[0], 1)
                    split(nxt())
                    tile(1)
                    dve.wait_ge(silu_ready, chunk + 1)
                    tt(T1[:, lo:T], SET[1][:, 0:cols], R[:, lo:T], ALU.mult).then_inc(t_free[1], 1)
                    dve.wait_ge(t_free[1], tiles[1].now())
                    tt(T2[:, lo:T], T2[:, lo:T], T1[:, lo:T], ALU.mult).then_inc(prod_ready, 1)
                    if lo_now:
                        hidden_lo(hs, chunk)

                def residual(k):
                    tile(k % 2)
                    stt(H[:, k, lo:T], SET[k % 2][:, 0:cols], 0.5, H[:, k, lo:T], ALU.mult, ALU.add).then_inc(t_free[k % 2], 1)

                gate_up(0, hid0, True)
                gate_up(2, hid0 + 1)
                with looped(dve, 0, (GROUPS - 1) // 2, ffn_counts(uses, tiles)) as t:
                    for g in range(2):
                        gate_up(1 - g, t * 4 + (hid0 + 2 * g + 2), lo_now=False)
                        for half in range(2):
                            split(nxt())
                            for q in range(4):
                                residual(4 * half + q)
                                if half == 0 and q == 0:
                                    hidden_lo(1 - g, t * 4 + (hid0 + 2 * g + 2))
                        gate_up(2, t * 4 + (hid0 + 2 * g + 3))
                def finished(k):
                    if gain is not None:
                        low_part(k, lo, gain, xcount + k + 1)
                    add_square(final_norm_, k, lo)
                    if not more:
                        if k == 0:
                            dve.wait_ge(sq_ready, KD * (final_norm_ - 1) + 1)
                        ts(H[:, k, lo:T], H[:, k, lo:T], COL[:, G_FIN + k:G_FIN + k + 1], None,
                           ALU.mult).then_inc(fin_ready, 1)

                for half in range(2):
                    if half == 0 or more:
                        split(nxt())
                    for k in range(4 * half, 4 * half + 4):
                        residual(k)
                        if not more:
                            finished(k)
                        elif k:
                            finished(k - 1)
                if more:
                    finished(KD - 1)

            for b in range(2):
                dve.sem_inc(c_free[b], 1)
            for i, t in enumerate(TOKEN_TILES):
                s = i % 2
                if s == 1:
                    tiles[s].add()
                    continue
                tile(s)
                n, a = (META, 0) if t < 0 else (P, META + t * P)
                nc.vector.tensor_copy(H[:, :, a:a + n], SET[s][:, 0:KD * n].rearrange("p (k n) -> p k n", k=KD)).then_inc(t_free[s], 1)
            tile(1)
            nc.vector.tensor_copy(COL[:], SET[1][:, 0:NVEC]).then_inc(t_free[1], 1)
            tile(0)
            nc.vector.tensor_copy(CWT[:].rearrange("p i t -> p (i t)"), SET[0][:, 0:4 * TAPS]).then_inc(t_free[0], 1)
            dve.wait_ge(masks_loaded, 16)
            nc.vector.tensor_copy(masks[:], MS[:]).then_inc(pad_set, 1)
            dve.wait_ge(t_free[1], tiles[1].now())
            split(FFN1_S0)
            mean_squares(0, 0)
            for k in range(KD):
                low_part(k, 0, G_FFN1, k + 1)
            tt(LBM[:], COL[:, LB0:LB0 + 8], COL[:, LB1:LB1 + 8], ALU.max).then_inc(lb_step, 1)
            dve.wait_ge(lb_step, 1)
            tt(LB[:], COL[:, LB0:LB0 + 8], LBM[:], ALU.subtract).then_inc(lb_step, 1)
            tt(OLB[:], COL[:, LB1:LB1 + 8], LBM[:], ALU.subtract).then_inc(lb_step, 1)
            dve.wait_ge(lb_exp, 2)
            tt(LBM[:], LB[:], OLB[:], ALU.add).then_inc(lb_step, 1)
            dve.wait_ge(lb_step, 4)
            nc.vector.reciprocal(LBM[:], LBM[:]).then_inc(lb_step, 1)
            dve.wait_ge(lb_step, 5)
            tt(LB[:], LB[:], LBM[:], ALU.mult).then_inc(lb_step, 1)
            tt(OLB[:], OLB[:], LBM[:], ALU.mult).then_inc(lb_step, 1)
            ffn(0, FFN1_S0, 0, 0, 1, G_MIX, KD, True)

            dve.wait_ge(h_saved, 16 * KD)
            nc.vector.memset(GLU[:, META + PROMPT:GLU_S], 0.0)
            nc.vector.memset(GLU[:, GLU_S + META + SAMPLE:GLU_LEN], 0.0).then_inc(pad_set, 1)

            def blocks_of(buf, lo, h):
                return buf[:, lo:T].rearrange("p (n two h) -> p n two h", two=2, h=h)

            def decays(l, direction):
                h = 1 << l
                nf, nb = (T if h <= META else DATA) // h, DATA // h
                if l == 0:
                    return FF[:, 0:T] if direction == 0 else FB[:, META:T]
                if l == 7:
                    return FL[:, direction, :]
                buf = KS if l % 2 else FF
                return buf[:, 0:nf] if direction == 0 else buf[:, nf:nf + nb]

            def raise_level(l):
                h = 1 << l
                for d, (A, B) in enumerate(((AF, BF), (AB, BB))):
                    F = decays(l, d)
                    with_meta = d == 0 and 2 * h <= META
                    if d == 0 and h == META:
                        F = F[:, 1:]
                    pairs = F.rearrange("p (n two) -> p n two", two=2)
                    skip = META // (2 * h) if with_meta else 0
                    far, near = (1, 0) if d == 0 else (0, 1)

                    def spread(half, a):
                        v = pairs[:, a:, half:half + 1]
                        return v.broadcast_to([P, v.shape[1], h]) if h > 1 else v

                    a = blocks_of(A, 0 if with_meta else META, h)[:, :, near, :]
                    tt(a, a, spread(far, 0), ALU.mult)
                    b = blocks_of(B, META, h)[:, :, far, :]
                    tt(b, b, spread(near, skip), ALU.mult)
                    up = tt(decays(l + 1, d), pairs[:, :, 0], pairs[:, :, 1], ALU.mult)
                return up

            three = lambda v: v.rearrange("p (c t) -> p c t", t=P)

            def rec(stage, h, taps_between):
                base = h * (PIECES // 2)

                def piece(name, n):
                    q = STAGE[name] + n
                    before = REC_BASE[q % 2] + q // 2
                    dve.wait_ge(c_full[q % 2], base + (before + 1))
                    return CB_[q % 2], c_free[q % 2], base + (before + 2)

                if stage == "v":
                    if not isinstance(h, int):
                        dve.wait_ge(y_ready, h)
                    for ready in (q_ready, f_ready, fb_ready, kf_ready, kb_ready):
                        dve.wait_ge(ready, h + 1)
                    tt(BF[:, META:T], Q[:, META:T], FF[:, META:T], ALU.mult)
                    tt(BB[:, META:T], Q[:, META:T], FB[:, META:T], ALU.mult)
                    tt(KS[:, META:T], AF[:, META:T], AB[:, META:T], ALU.add).then_inc(bks_ready, 1)
                if stage == 0:
                    dve.wait_ge(sc_free, h + 1)
                    taps_between(1)
                    for n, (c0, c1) in enumerate(CHUNK_PIECES):
                        bank, free, _ = piece("diag", n)
                        tt(three(SC[:, META + c0 * P:META + c1 * P]), three(bank[:, 0:(c1 - c0) * P]),
                           ident[:].rearrange("p (c t) -> p c t", c=1).broadcast_to([P, c1 - c0, P]),
                           ALU.mult).then_inc(free, 1)
                raise_first = stage in range(1, len(LEVELS))
                if raise_first:
                    taps_between(1)
                    dve.wait_ge(merged, (len(LEVELS) - 1) * h + stage)
                    raise_level(stage).then_inc(level_up, 1)
                if stage in range(len(LEVELS)):
                    for n, (c0, c1) in enumerate(CHUNK_PIECES):
                        if n == 2:
                            taps_between(1)
                        bank, free, _ = piece(LEVELS[stage], n)
                        dve.sem_inc(dve_passed, 1)
                        nc.vector.copy_predicated(three(SC[:, META + c0 * P:META + c1 * P]),
                                                  masks[:, stage:stage + 1, :].broadcast_to([P, c1 - c0, P]),
                                                  three(bank[:, 0:(c1 - c0) * P])).then_inc(free, 1)
                    if not raise_first:
                        if stage:
                            dve.wait_ge(level_up, 7 * h + stage)
                        else:
                            dve.wait_ge(bks_ready, h + 1)
                        raise_level(stage).then_inc(level_up, 1)
                if stage == 8:
                    prev = (level_up, 7 * h + 7)
                    steps = 0
                    for n, gs in enumerate(G_PIECES):
                        bank, free, freed = piece("g", n)
                        for j, (d, c) in enumerate(gs):
                            g = bank[:, j * P:(j + 1) * P]
                            last = j == len(gs) - 1
                            dve.wait_ge(*prev)
                            if c == "meta" or (d, c) in (("b", PCH - 1), ("b", NCH - 1)):
                                dst = KS[:, 0:P] if d == "f" else AF[:, (c - 1) * P:c * P]
                                ins = nc.vector.tensor_copy(dst, g)
                            elif d == "f":
                                ins = stt(KS[:, (c + 1) * P:(c + 2) * P], KS[:, state_f(c) * P:(state_f(c) + 1) * P],
                                          FL[:, 0, c:c + 1], g, ALU.mult, ALU.add)
                            else:
                                ins = stt(AF[:, (c - 1) * P:c * P], AF[:, c * P:(c + 1) * P], FL[:, 1, c:c + 1], g,
                                          ALU.mult, ALU.add)
                            if last:
                                ins.then_inc(free, 1)
                                prev = (free, freed)
                            else:
                                ins.then_inc(state_step, 1)
                                steps += 1
                                prev = (state_step, h * (len(ALL_G) - len(G_PIECES)) + steps)
                if stage == 10:
                    taps_between(1)
                    bank, free, freed = piece("ss", 0)
                    ts(RH[:], bank[:, 0:NCH], 1.0 / P, RMS_EPS, ALU.mult, ALU.add).then_inc(free, 1)
                    dve.wait_ge(free, freed)
                    dve.sem_inc(hms_ready, 1)
                if stage == 11:
                    taps_between(1)
                    dve.wait_ge(orms_ready, h + 1)
                    nc.vector.reciprocal(RH[:], RH[:]).then_inc(ors_ready, 1)
                    dve.wait_ge(ors_ready, h + 1)
                    diagonals(KS, RH[:], hdiag_ready)
                if stage == 12:
                    hgn = COL[:, HGN + h:HGN + h + 1] if isinstance(h, int) else COL[:, bass.ds(h + HGN, 1)]
                    for n, (a, b) in enumerate(COL_PIECES):
                        bank, free, freed = piece("rb", n)
                        o = BF[:, META + a:META + b]
                        stt(o, o, hgn, bank[:, 0:b - a], ALU.mult, ALU.mult).then_inc(free, 1)
                    dve.wait_ge(free, freed)
                    y = YB[:, h, META:T] if isinstance(h, int) else SC[:, META:T]
                    tt(y, BF[:, META:T], GS[:, META:T], ALU.mult).then_inc(y_ready, 1)

            def tap(i, j):
                src = GLU[:, 1 + j:1 + j + COUT_LEN]
                w = (CWT[:, i, j:j + 1] if isinstance(i, int) else
                     CWT[:, bass.ds(i, 1), j:j + 1].rearrange("p a t -> p (a t)"))
                if j == 0:
                    dve.wait_ge(glu_ready, i + 1)
                    dve.wait_ge(c_saved, i * 32)
                    cb = COL[:, CB + i:CB + i + 1] if isinstance(i, int) else COL[:, bass.ds(i + CB, 1)]
                    ts(COUT[:, 0:COUT_LEN], src, w, cb, ALU.mult, ALU.add).then_inc(tap_done, 1)
                else:
                    dve.wait_ge(tap_done, i * (TAPS - 1) + j)
                    stt(COUT[:, 0:COUT_LEN], src, w, COUT[:, 0:COUT_LEN], ALU.mult, ALU.add)\
                        .then_inc(conv_ready if j == TAPS - 1 else tap_done, 1)

            def evacuate(i, pos, taps_between):
                s = pos % 2
                lo = META if pos in (3, 5, 6) else 0
                tile(s)
                if pos == 5:
                    dve.wait_ge(kf_raw, i + 1)
                if pos == 6:
                    dve.wait_ge(kb_raw, i + 1)
                out = T2 if pos == 1 else VT if pos == 2 else T1
                tt(out[:, lo:T], SET[s][:, 0:T - lo], R[:, lo:T], ALU.mult).then_inc(t_free[s], 1)
                if pos not in (0, 2):
                    taps_between(2)
                if pos == 1:
                    if not isinstance(i, int):
                        dve.wait_ge(conv_ready, i)
                    dve.wait_ge(glu_sig, i + 1)
                    tt(GLU[:, 0:META + PROMPT], T1[:, 0:META + PROMPT], T2[:, 0:META + PROMPT], ALU.mult)
                    tt(GLU[:, GLU_S:GLU_S + META], T1[:, 0:META], T2[:, 0:META], ALU.mult)
                    tt(GLU[:, GLU_S + META:GLU_S + META + SAMPLE], T1[:, META + PROMPT:T], T2[:, META + PROMPT:T],
                       ALU.mult).then_inc(glu_ready, 1)
                if pos == 3:
                    dve.wait_ge(q_sig, i + 1)
                    tt(Q[:, lo:T], T1[:, lo:T], T2[:, lo:T], ALU.mult).then_inc(q_ready, 1)
                if pos in (4, 5):
                    sig, F, ready, ld = ((f_sig, FF, f_ready, 0), (fb_sig, FB, fb_ready, HEADS))[pos - 4]
                    dve.wait_ge(sig, i + 1)
                    olb, lb = ((v[:, i + ld:i + ld + 1] if isinstance(i, int) else v[:, bass.ds(i + ld, 1)])
                               for v in (OLB, LB))
                    ts(F[:, lo:T], T2[:, lo:T], olb, lb, ALU.mult, ALU.add).then_inc(ready, 1)
                if pos == 6:
                    dve.wait_ge(g_sig, i + 1)
                    tt(GS[:, lo:T], T1[:, lo:T], T2[:, lo:T], ALU.mult)

            def head(i, z, r):
                for slot in range(14):
                    pos = slot // 2
                    chunk, counts, j0 = (i - 1, TAPS_BEFORE, sum(TAPS_NOW.values())) if slot < 4 else (i, TAPS_NOW, 0)
                    left = [j0 + sum(counts[a] for a in counts if a < slot),
                            j0 + sum(counts[a] for a in counts if a <= slot)]
                    if (slot < 4 and not r) or (slot >= 4 and not z):
                        left = [0, 0]

                    def taps_between(n):
                        for _ in range(min(n, left[1] - left[0])):
                            tap(chunk, left[0])
                            left[0] += 1

                    if z and slot % 2 == 0:
                        split((HEAD_SLOTS + HEAD_SLOTS[0:1])[pos + 1])
                    if r:
                        rec(slot, i - 1, taps_between)
                    if z and slot == 13:
                        rec("v", i, taps_between)
                    if slot in (7, 9):
                        taps_between(2)
                    if z and slot % 2:
                        if z == "first" and pos == 1:
                            make_r(1, 0)
                            evacuate(i, 0, taps_between)
                        if not (z == "first" and pos == 0):
                            evacuate(i, pos, taps_between)
                        else:
                            mean_squares(1, 0)
                    taps_between(TAPS)

            dve.wait_ge(pad_set, 2)
            head(0, "first", False)
            with looped(dve, 1, HEADS, head_counts(uses, tiles)) as i:
                head(i, "z", True)

            def lo_part(n, src, count):
                dve.wait_ge(xh_ready, 2 * KD + count)
                tt(XL[:, n, META:T], src, XH[:, n, META:T].bitcast(F32), ALU.subtract).then_inc(xl_ready, 1)

            def less_mean(ns):
                for n in ns:
                    stt(CR[:, n, META:T], SET[0][:, 0:DATA], -1.0 / W, CR[:, n, META:T], ALU.mult, ALU.add)\
                        .then_inc(cxc if n < 3 else t_free[0], 1)

            def over_deviation(ns):
                for n in ns:
                    tt(CR[:, n, META:T], CR[:, n, META:T], SET[0][:, 0:DATA], ALU.mult).then_inc(cn if n < 3 else t_free[0], 1)

            at_tap = [sum(TAPS_NOW.values())]
            for slot in range(14):
                stop = at_tap[0] + TAPS_LAST.get(slot, 0)

                def taps_between(n):
                    for _ in range(min(n, stop - at_tap[0])):
                        tap(HEADS - 1, at_tap[0])
                        at_tap[0] += 1

                if slot == 8:
                    dve.wait_ge(croot_ready, 1)
                    nc.vector.reciprocal(RS[:, 0:NCH], RS[:, 0:NCH]).then_inc(cinv_ready, 1)
                    dve.wait_ge(cinv_ready, 1)
                    diagonals(T1, RS[:, 0:NCH], cdiag_ready)
                rec(slot, HEADS - 1, taps_between)
                taps_between(TAPS)
                if slot in (0, 1):
                    split(EARLY_SLOTS[slot + 1])
                if slot in (1, 2):
                    for n in ((0,), (1, 2))[slot - 1]:
                        lo_part(n, YB[:, n, META:T], n + 1)
                if slot in EARLY_OUT:
                    n, s = EARLY_OUT[slot]
                    tile(s)
                    dve.wait_ge(h_back[n], 16)
                    tt(RESIDUAL[n], SET[s][:, 0:DATA], RESIDUAL[n], ALU.add).then_inc(t_free[s], 1)
                if slot == 4:
                    tile(0)
                    less_mean((0, 1))
                if slot == 5:
                    less_mean((2, 3))
                if slot == 6:
                    for n in (0, 2):
                        dve.wait_ge(csq, n + 2)
                        tt(CSQ[:, n, META:T], CSQ[:, n, META:T], CSQ[:, n + 1, META:T], ALU.add).then_inc(csq_added, 1)
                    dve.wait_ge(csq_added, 2)
                    tt(CSQ[:, 0, META:T], CSQ[:, 0, META:T], CSQ[:, 2, META:T], ALU.add).then_inc(csq_added, 1)
                if slot == 7:
                    tile(0)
                    ts(RS[:, 0:NCH], SET[0][:, 0:NCH], 1.0 / W, LN_EPS, ALU.mult, ALU.add).then_inc(t_free[0], 1)
                    dve.wait_ge(t_free[0], tiles[0].now())
                    dve.sem_inc(cms_ready, 1)
                if slot == 8:
                    tile(0)
                    over_deviation((0, 1))
                if slot == 9:
                    over_deviation((2, 3))
                if slot in (10, 11):
                    for n in ((0, 1), (2, 3))[slot - 10]:
                        lo_part(HEADS + n, CR[:, n, META:T], EARLY + n + 1)
            for b in range(2):
                pieces[b].add(HEADS * PIECES // 2)
            for n in range(2):
                split(OUT_SLOTS[n], LATE * P)
            lo_part(EARLY, YB[:, EARLY, META:T], KD)
            for n in range(KD):
                if n + 2 < KD:
                    split(OUT_SLOTS[n + 2], LATE * P)
                elif n + 2 == KD:
                    split(FFN2_S0)
                tile(n % 2)
                tt(H[:, n, META:T], SET[n % 2][:, 0:DATA], RESIDUAL[n], ALU.add).then_inc(t_free[n % 2], 1)
                if n:
                    add_square(2, n - 1, META)
            for k in range(KD):
                low_part(k, META, G_FFN2, 3 * KD + k + 1)
                if k == 1:
                    add_square(2, KD - 1, META)
            ffn(META, FFN2_S0, NF, 2, 3, None, 0, False)
            for b in range(2):
                pieces[b].add(3 * KD // 2)
            mean_squares(3, META)
            inverse(3, META)
            for t in range(0, NCH, 2):
                if t == 0:
                    for b in range(2):
                        dve.wait_ge(c_free[b], pieces[b].now(1))
                ts(XO[:, t, :], XO[:, t, :], RS[:, t:t + 1], None, ALU.mult).then_inc(xo_ready[0], 1)


SBUF_BASE, SBUF_TOP = 16512, 229312


def level_masks():
    s, t = np.arange(P)[:, None], np.arange(P)[None, :]
    return np.stack([(s // (2 * h) == t // (2 * h)) & (s // h != t // h) for h in LEVELS], 1).astype(np.float32)


_INS = ["x_prompt", "x_sample", "meta_tokens", "ffn1_norm", "ffn1_w_gate", "ffn1_w_up", "ffn1_w_down", "mix_norm",
        "w_in", "lb_logits", "hg_norm", "conv_w", "conv_b", "conv_ln_g", "conv_ln_b", "w_out", "ffn2_norm",
        "ffn2_w_gate", "ffn2_w_up", "ffn2_w_down", "final_norm"]


def kernel(**inputs):
    import concourse.bacc as bacc
    from concourse.bass_utils import run_bass_kernel_spmd

    nc = bacc.Bacc("TRN2", target_bir_lowering=False, num_devices=1)
    arrays = {name: np.ascontiguousarray(inputs[name]) for name in _INS}
    arrays["identity"] = np.eye(P, dtype=np.float32)
    arrays["level_masks"] = level_masks()
    args = [nc.dram_tensor(f"in_{n}", a.shape, mybir.dt.from_np(a.dtype), kind="ExternalInput").ap()
            for n, a in arrays.items()]
    outs = [nc.dram_tensor(f"out_{n}", (1, rows, D), F32, kind="ExternalOutput").ap()
            for n, rows in (("prompt", PROMPT), ("sample", SAMPLE))]
    encoder(nc, *args, *outs)
    r = run_bass_kernel_spmd(nc, [{f"in_{n}": a for n, a in arrays.items()}], core_ids=[0])
    return tuple(r.results[0][f"out_{n}"] for n in ("prompt", "sample"))
```
